# Optimizing a Trainium2 kernel written in Bass

```python
import math
import jax, jax.numpy as jnp
from jax import lax
import numpy as np

D_MODEL = 1024
BATCH = 1
SEQ = 512
DEPTH = 1

Q_BLOCK = 128
EPS = 1e-6
MLA_HEADS = 8
MLA_Q_LORA = 384
MLA_KV_LORA = 256
MLA_NOPE = 128
MLA_ROPE = 64
MLA_V = 128
ROPE_BASE = 10000.0
DSA_HEADS = 8
DSA_HEAD_DIM = 128
IDX_HEADS = 8
IDX_DIM = 64
DSA_TOPK_MAX = 256
NSA_HEADS = 8
NSA_GROUPS = 2
NSA_HEAD_DIM = 128
CMP_STRIDE = 16
CMP_LEN = 2 * CMP_STRIDE
CMP_HIDDEN = 256
SEL_BLOCK = 64
SEL_COUNT = 16
WINDOW = 512
REL_BUCKETS = 32
REL_MAX_DIST = 128
REL_HEADS = DSA_HEADS + NSA_HEADS
MEM_LEN = 256
CROSS_HEADS = 4
CROSS_HEAD_DIM = D_MODEL // CROSS_HEADS
D_FF = 4 * D_MODEL
N_BRANCH = 3
BRANCH_WIDTH = D_MODEL
NORM_PRE_MIX, NORM_POST_MIX, NORM_PRE_CROSS, NORM_MEM, NORM_POST_CROSS, NORM_PRE_MLP, NORM_POST_MLP = 0, 1, 2, 3, 4, 5, 6
N_NORMS = 7
IN_WIDTHS = (
    MLA_Q_LORA, MLA_KV_LORA, MLA_ROPE,
    DSA_HEADS * DSA_HEAD_DIM, DSA_HEADS * DSA_HEAD_DIM, DSA_HEADS * DSA_HEAD_DIM,
    IDX_HEADS * IDX_DIM, IDX_DIM, IDX_HEADS,
    NSA_HEADS * NSA_HEAD_DIM,
    NSA_GROUPS * NSA_HEAD_DIM, NSA_GROUPS * NSA_HEAD_DIM,
    NSA_GROUPS * NSA_HEAD_DIM, NSA_GROUPS * NSA_HEAD_DIM,
    NSA_GROUPS * NSA_HEAD_DIM, NSA_GROUPS * NSA_HEAD_DIM,
    3 * NSA_HEADS,
    N_BRANCH * D_MODEL,
)
D_IN = sum(IN_WIDTHS)

kernel_name = 'hybrid_mla_dsa_nsa_gated_block'

def split_cols(p):
    offs = np.cumsum(IN_WIDTHS)[:-1].tolist()
    return jnp.split(p, offs, axis=-1)

def rmsnorm(x, g):
    xf = x.astype(jnp.float32)
    y = xf * lax.rsqrt(jnp.mean(xf * xf, axis=-1, keepdims=True) + EPS)
    return (y * g.astype(jnp.float32)).astype(x.dtype)

def masked_softmax(s, mask):
    s = jnp.where(mask, s.astype(jnp.float32), -jnp.inf)
    m = jnp.max(s, axis=-1, keepdims=True)
    m = jnp.where(jnp.isfinite(m), m, 0.0)
    p = jnp.exp(s - m)
    d = jnp.sum(p, axis=-1, keepdims=True)
    return p / jnp.where(d > 0, d, 1.0)

def rel_bucket(dist):
    n = jnp.maximum(dist, 0)
    exact = REL_BUCKETS // 2
    nf = jnp.maximum(n, 1).astype(jnp.float32)
    log_b = exact + (jnp.log(nf / exact) / math.log(REL_MAX_DIST / exact) * (REL_BUCKETS - exact)).astype(jnp.int32)
    return jnp.where(n < exact, n, jnp.minimum(log_b, REL_BUCKETS - 1))

def rope(x, cos, sin):
    x1, x2 = jnp.split(x.astype(jnp.float32), 2, axis=-1)
    return jnp.concatenate([x1 * cos - x2 * sin, x2 * cos + x1 * sin], axis=-1).astype(x.dtype)

def sweep_query_blocks(fn, seq):
    out = lax.map(fn, jnp.arange(seq // Q_BLOCK))
    return jax.tree_util.tree_map(
        lambda a: jnp.moveaxis(a, 0, 1).reshape((a.shape[1], seq) + a.shape[3:]), out)

def mla(q_lat, kv_lat, k_rope, positions, q_norm, kv_norm, w_uq, w_ukv):
    B, S, _ = q_lat.shape
    q = (rmsnorm(q_lat, q_norm) @ w_uq).reshape(B, S, MLA_HEADS, MLA_NOPE + MLA_ROPE)
    kv = (rmsnorm(kv_lat, kv_norm) @ w_ukv).reshape(B, S, MLA_HEADS, MLA_NOPE + MLA_V)
    q_nope, q_rope = q[..., :MLA_NOPE], q[..., MLA_NOPE:]
    k_nope, v = kv[..., :MLA_NOPE], kv[..., MLA_NOPE:]
    inv_freq = ROPE_BASE ** (-jnp.arange(0, MLA_ROPE, 2, dtype=jnp.float32) / MLA_ROPE)
    ang = positions.astype(jnp.float32)[..., None] * inv_freq
    cos, sin = jnp.cos(ang), jnp.sin(ang)
    q_rope = rope(q_rope, cos[:, :, None], sin[:, :, None])
    k_rope = rope(k_rope, cos, sin)
    scale = (MLA_NOPE + MLA_ROPE) ** -0.5
    kpos = jnp.arange(S)

    def block(i):
        t0 = i * Q_BLOCK
        qn = lax.dynamic_slice_in_dim(q_nope, t0, Q_BLOCK, axis=1)
        qr = lax.dynamic_slice_in_dim(q_rope, t0, Q_BLOCK, axis=1)
        s = jnp.einsum('bthd,bshd->bhts', qn, k_nope) + jnp.einsum('bthr,bsr->bhts', qr, k_rope)
        t = t0 + jnp.arange(Q_BLOCK)
        p = masked_softmax(s * scale, kpos[None, :] <= t[:, None]).astype(v.dtype)
        return jnp.einsum('bhts,bshd->bthd', p, v)

    return sweep_query_blocks(block, S).reshape(B, S, MLA_HEADS * MLA_V)

def dsa(q, k, v, iq, ik, iw, tab):
    B, S, _ = q.shape
    q = q.reshape(B, S, DSA_HEADS, DSA_HEAD_DIM)
    k = k.reshape(B, S, DSA_HEADS, DSA_HEAD_DIM)
    v = v.reshape(B, S, DSA_HEADS, DSA_HEAD_DIM)
    iq = iq.reshape(B, S, IDX_HEADS, IDX_DIM)
    topk = min(DSA_TOPK_MAX, S // 4)
    scale = DSA_HEAD_DIM ** -0.5
    kpos = jnp.arange(S)
    gather = jax.vmap(lambda arr, ids: arr[ids])

    def block(i):
        t0 = i * Q_BLOCK
        t = t0 + jnp.arange(Q_BLOCK)
        qb = lax.dynamic_slice_in_dim(q, t0, Q_BLOCK, axis=1)
        iqb = lax.dynamic_slice_in_dim(iq, t0, Q_BLOCK, axis=1)
        iwb = lax.dynamic_slice_in_dim(iw, t0, Q_BLOCK, axis=1)
        score = jnp.einsum('bth,bths->bts', iwb, jax.nn.relu(jnp.einsum('bthd,bsd->bths', iqb, ik)))
        score = jnp.where(kpos[None, :] <= t[:, None], score.astype(jnp.float32), -jnp.inf)
        _, idx = lax.top_k(score, topk)
        valid = idx <= t[None, :, None]
        kg = gather(k, idx)
        vg = gather(v, idx)
        bias = tab[rel_bucket(t[None, :, None] - idx)]
        s = jnp.einsum('bthd,btkhd->bhtk', qb, kg) * scale + jnp.transpose(bias, (0, 3, 1, 2))
        p = masked_softmax(s, valid[:, None]).astype(v.dtype)
        return jnp.einsum('bhtk,btkhd->bthd', p, vg)

    return sweep_query_blocks(block, S).reshape(B, S, DSA_HEADS * DSA_HEAD_DIM)

def nsa(q, kc, vc, ks, vs, kw, vw, gate, cmp_pos, cmp_w1, cmp_w2, tab):
    B, S, _ = q.shape
    G, HG, dk = NSA_GROUPS, NSA_HEADS // NSA_GROUPS, NSA_HEAD_DIM
    q = q.reshape(B, S, G, HG, dk)
    scale = dk ** -0.5
    t_all = jnp.arange(S)

    def compress(a, pos, w1, w2):
        a = a.reshape(B, S // CMP_STRIDE, CMP_STRIDE, G, dk)
        blocks = jnp.concatenate([a[:, :-1], a[:, 1:]], axis=2) + pos[None, None, :, None, :]
        nc_ = blocks.shape[1]
        flat = jnp.transpose(blocks, (0, 1, 3, 2, 4)).reshape(B, nc_, G, CMP_LEN * dk)
        return jax.nn.gelu(flat @ w1) @ w2

    k_cmp = compress(kc, cmp_pos[0], cmp_w1[0], cmp_w2[0])
    v_cmp = compress(vc, cmp_pos[1], cmp_w1[1], cmp_w2[1])
    nc = S // CMP_STRIDE - 1
    c_start = jnp.arange(nc) * CMP_STRIDE
    cmask = (c_start + CMP_LEN - 1)[None, :] <= t_all[:, None]
    p_c = masked_softmax(jnp.einsum('btghd,bcgd->bghtc', q, k_cmp) * scale, cmask)
    o_c = jnp.einsum('bghtc,bcgd->btghd', p_c.astype(v_cmp.dtype), v_cmp)

    ns = S // SEL_BLOCK
    j = jnp.arange(ns)
    j_start = j * SEL_BLOCK
    overlap = ((c_start[:, None] < j_start[None, :] + SEL_BLOCK) &
               (c_start[:, None] + CMP_LEN > j_start[None, :])).astype(jnp.float32)
    imp = jnp.einsum('bghtc,cj->bgtj', p_c, overlap)
    blk_t = t_all // SEL_BLOCK
    forced = (j[None, :] == 0) | (j[None, :] == blk_t[:, None]) | (j[None, :] == blk_t[:, None] - 1)
    imp = jnp.where(forced, jnp.inf, imp)
    imp = jnp.where(j_start[None, :] > t_all[:, None], -jnp.inf, imp)
    n_sel = min(SEL_COUNT, ns)
    _, sel_idx = lax.top_k(imp, n_sel)
    ks_blocks = jnp.transpose(ks.reshape(B, ns, SEL_BLOCK, G, dk), (0, 3, 1, 2, 4))
    vs_blocks = jnp.transpose(vs.reshape(B, ns, SEL_BLOCK, G, dk), (0, 3, 1, 2, 4))
    gather_blocks = jax.vmap(jax.vmap(lambda blk, ids: blk[ids]))

    pad = ((0, 0), (WINDOW, 0), (0, 0), (0, 0))
    kw_pad = jnp.pad(kw.reshape(B, S, G, dk), pad)
    vw_pad = jnp.pad(vw.reshape(B, S, G, dk), pad)

    tab_g = jnp.transpose(tab.reshape(REL_BUCKETS, G, HG), (1, 0, 2))
    g_idx = jnp.arange(G)[None, :, None, None]
    n_keys_sel = n_sel * SEL_BLOCK

    def block(i):
        t0 = i * Q_BLOCK
        tq = t0 + jnp.arange(Q_BLOCK)
        qb = lax.dynamic_slice_in_dim(q, t0, Q_BLOCK, axis=1)
        idx = lax.dynamic_slice_in_dim(sel_idx, t0, Q_BLOCK, axis=2)
        kg = gather_blocks(ks_blocks, idx).reshape(B, G, Q_BLOCK, n_keys_sel, dk)
        vg = gather_blocks(vs_blocks, idx).reshape(B, G, Q_BLOCK, n_keys_sel, dk)
        kpos = (idx[..., None] * SEL_BLOCK + jnp.arange(SEL_BLOCK)).reshape(B, G, Q_BLOCK, n_keys_sel)
        dist = tq[None, None, :, None] - kpos
        bias = tab_g[g_idx, rel_bucket(dist)]
        s = jnp.einsum('btghd,bgtkd->bghtk', qb, kg) * scale + jnp.transpose(bias, (0, 1, 4, 2, 3))
        p = masked_softmax(s, (dist >= 0)[:, :, None]).astype(vg.dtype)
        o_s = jnp.einsum('bghtk,bgtkd->btghd', p, vg)
        kwin = lax.dynamic_slice_in_dim(kw_pad, t0, WINDOW + Q_BLOCK, axis=1)
        vwin = lax.dynamic_slice_in_dim(vw_pad, t0, WINDOW + Q_BLOCK, axis=1)
        spos = t0 - WINDOW + jnp.arange(WINDOW + Q_BLOCK)
        wd = tq[:, None] - spos[None, :]
        wmask = (wd >= 0) & (wd < WINDOW) & (spos[None, :] >= 0)
        wbias = jnp.transpose(tab_g[:, rel_bucket(wd)], (0, 3, 1, 2))[None]
        s_w = jnp.einsum('btghd,bsgd->bghts', qb, kwin) * scale + wbias
        p_w = masked_softmax(s_w, wmask).astype(vwin.dtype)
        o_w = jnp.einsum('bghts,bsgd->btghd', p_w, vwin)
        return o_s, o_w

    o_s, o_w = sweep_query_blocks(block, S)
    gt = jax.nn.sigmoid(gate.reshape(B, S, 3, G, HG))[..., None]
    o = gt[:, :, 0] * o_c + gt[:, :, 1] * o_s + gt[:, :, 2] * o_w
    return o.reshape(B, S, NSA_HEADS * dk)

def cross_attn(h, m, wq, wkv, wo):
    B, S, _ = h.shape
    q = (h @ wq).reshape(B, S, CROSS_HEADS, CROSS_HEAD_DIM)
    kv = (m @ wkv).reshape(B, m.shape[1], 2, CROSS_HEADS, CROSS_HEAD_DIM)
    k, v = kv[:, :, 0], kv[:, :, 1]
    s = jnp.einsum('bthd,bmhd->bhtm', q, k) * CROSS_HEAD_DIM ** -0.5
    p = jax.nn.softmax(s.astype(jnp.float32), axis=-1).astype(v.dtype)
    return jnp.einsum('bhtm,bmhd->bthd', p, v).reshape(B, S, D_MODEL) @ wo

def setup_inputs(seed: int = 0) -> dict:
    key = jax.random.key(seed)
    ks = jax.random.split(key, 20)
    f32 = jnp.float32

    def nrm(k, shape):
        return jax.random.normal(k, shape, f32)

    def w(k, shape, fan_in):
        return nrm(k, shape) * fan_in ** -0.5

    dk = NSA_HEAD_DIM
    return {
        'x': nrm(ks[0], (BATCH, SEQ, D_MODEL)),
        'mem': nrm(ks[1], (BATCH, MEM_LEN, D_MODEL)),
        'positions': jnp.tile(jnp.arange(SEQ, dtype=jnp.int32)[None, :], (BATCH, 1)),
        'rel_bias': 0.5 * nrm(ks[2], (REL_BUCKETS, REL_HEADS)),
        'norm_gains': 1.0 + 0.05 * nrm(ks[3], (DEPTH, N_NORMS, D_MODEL)),
        'w_in': w(ks[4], (DEPTH, D_MODEL, D_IN), D_MODEL),
        'mla_q_norm': 1.0 + 0.05 * nrm(ks[5], (DEPTH, MLA_Q_LORA)),
        'mla_kv_norm': 1.0 + 0.05 * nrm(ks[6], (DEPTH, MLA_KV_LORA)),
        'mla_w_uq': w(ks[7], (DEPTH, MLA_Q_LORA, MLA_HEADS * (MLA_NOPE + MLA_ROPE)), MLA_Q_LORA),
        'mla_w_ukv': w(ks[8], (DEPTH, MLA_KV_LORA, MLA_HEADS * (MLA_NOPE + MLA_V)), MLA_KV_LORA),
        'nsa_cmp_pos': 0.5 * nrm(ks[9], (DEPTH, 2, CMP_LEN, dk)),
        'nsa_cmp_w1': w(ks[10], (DEPTH, 2, CMP_LEN * dk, CMP_HIDDEN), CMP_LEN * dk),
        'nsa_cmp_w2': w(ks[11], (DEPTH, 2, CMP_HIDDEN, dk), CMP_HIDDEN),
        'w_branch': w(ks[12], (DEPTH, N_BRANCH, BRANCH_WIDTH, D_MODEL), BRANCH_WIDTH),
        'w_out': w(ks[13], (DEPTH, D_MODEL, D_MODEL), D_MODEL),
        'cross_wq': w(ks[14], (DEPTH, D_MODEL, D_MODEL), D_MODEL),
        'cross_wkv': w(ks[15], (DEPTH, D_MODEL, 2 * D_MODEL), D_MODEL),
        'cross_wo': w(ks[16], (DEPTH, D_MODEL, D_MODEL), D_MODEL),
        'mlp_w1': w(ks[17], (DEPTH, D_MODEL, D_FF), D_MODEL),
        'mlp_w2': w(ks[18], (DEPTH, D_FF, D_MODEL), D_FF),
    }

def reference(x, mem, positions, rel_bias, norm_gains, w_in, mla_q_norm, mla_kv_norm,
              mla_w_uq, mla_w_ukv, nsa_cmp_pos, nsa_cmp_w1, nsa_cmp_w2, w_branch, w_out,
              cross_wq, cross_wkv, cross_wo, mlp_w1, mlp_w2):
    B, S, _ = x.shape
    tab_dsa = rel_bias[:, :DSA_HEADS]
    tab_nsa = rel_bias[:, DSA_HEADS:]
    for l in range(DEPTH):
        g = norm_gains[l]
        h = rmsnorm(x, g[NORM_PRE_MIX])
        (mla_q_lat, mla_kv_lat, mla_k_rope, dsa_q, dsa_k, dsa_v, idx_q, idx_k, idx_w,
         nsa_q, nsa_kc, nsa_vc, nsa_ks, nsa_vs, nsa_kw, nsa_vw, nsa_gate, branch_gate) = split_cols(h @ w_in[l])
        o_a = mla(mla_q_lat, mla_kv_lat, mla_k_rope, positions, mla_q_norm[l], mla_kv_norm[l],
                  mla_w_uq[l], mla_w_ukv[l])
        o_b = dsa(dsa_q, dsa_k, dsa_v, idx_q, idx_k, idx_w, tab_dsa)
        o_c = nsa(nsa_q, nsa_kc, nsa_vc, nsa_ks, nsa_vs, nsa_kw, nsa_vw, nsa_gate,
                  nsa_cmp_pos[l], nsa_cmp_w1[l], nsa_cmp_w2[l], tab_nsa)
        gates = jax.nn.sigmoid(branch_gate.reshape(B, S, N_BRANCH, D_MODEL))
        merged = (gates[:, :, 0] * (o_a @ w_branch[l, 0]) +
                  gates[:, :, 1] * (o_b @ w_branch[l, 1]) +
                  gates[:, :, 2] * (o_c @ w_branch[l, 2]))
        x = x + rmsnorm(merged @ w_out[l], g[NORM_POST_MIX])
        h = rmsnorm(x, g[NORM_PRE_CROSS])
        m = rmsnorm(mem, g[NORM_MEM])
        x = x + rmsnorm(cross_attn(h, m, cross_wq[l], cross_wkv[l], cross_wo[l]), g[NORM_POST_CROSS])
        h = rmsnorm(x, g[NORM_PRE_MLP])
        x = x + rmsnorm(jnp.square(jax.nn.relu(h @ mlp_w1[l])) @ mlp_w2[l], g[NORM_POST_MLP])
    return x


_drawn_inputs = setup_inputs


def setup_inputs(seed=0):
    import zlib

    import numpy as np

    out = dict(_drawn_inputs(seed))
    spreads = {}
    factors = {'mla_q_norm': 3.792, 'mla_kv_norm': 2.708}
    for name, (base, spread) in spreads.items():
        noise = np.random.default_rng([zlib.crc32(name.encode()), seed]).standard_normal(out[name].shape)
        drawn = base * np.exp(spread * noise) if base else spread * noise
        out[name] = __import__('jax').numpy.asarray(drawn.astype(out[name].dtype))
    for name, factor in factors.items():
        out[name] = (out[name] * factor).astype(out[name].dtype)
    return out
```

```python
from contextlib import ExitStack

import numpy as np
import concourse.bass as bass
import concourse.mybir as mybir

F32 = mybir.dt.float32
F32R = mybir.dt.float32r
I32 = mybir.dt.int32
ALU = mybir.AluOpType
ACT = mybir.ActivationFunctionType
AX = mybir.AxisListType.X

P = 128
T = 512
NT = T // P
D = 1024
KD = D // P
EPS = 1e-6
NEG = -1e30
FILL = -3e38
TOPK = 128
DQ, DKV, ROPE = 384, 256, 64
MLA_SCALE = (128 + ROPE) ** -0.5
HEAD_SCALE = 128 ** -0.5
CROSS_SCALE = 256 ** -0.5
MEM = 256
NC = T // 16 - 1
FF = 4 * D
SW = 256
GROUPS = D // SW
WIDTHS = (DQ, DKV, ROPE, D, D, D, 512, 64, 8, D, 256, 256, 256, 256, 256, 256, 24, 3 * D)
COLS = [sum(WIDTHS[:i]) for i in range(len(WIDTHS))]
(C_LAT, _, _, C_DQ, C_DK, C_DV, C_IQ, C_IK, _, C_NQ, C_KC, C_VC, C_KS, C_VS, C_KW, C_VW, C_NG,
 C_BG) = COLS
TRI = [P * sum(range(1, i + 1)) for i in range(NT)]
UNIT = P * NT * (NT + 1) // 2


def shape_constants():
    n = np.arange(T - 1, -1, -1)
    exact = 16
    far = exact + (np.log(np.maximum(n, 1) / exact) / np.log(128 / exact) * exact).astype(np.int64)
    bucket = np.where(n < exact, n, np.minimum(far, 31))
    onehot = (bucket[None, :] == np.arange(32)[:, None]).astype(np.float32)
    row = np.arange(P)
    freq = np.float32(10000.0) ** (-(np.arange(0, ROPE, 2, dtype=np.float32)) / np.float32(ROPE))
    turn = np.stack([freq[row % 32], np.where(row % 64 < 32, -1.0, 1.0)], 1).astype(np.float32)
    strip = np.zeros((P, T), np.float32)
    strip[:, T - P:] = np.where(row[None, :] > row[:, None], NEG, 0.0)
    t = np.arange(T).reshape(NT, P).T
    late = (np.arange(NC) * 16 + 31)[None, None, :] > t[:, :, None]
    return {
        "c_ident": np.eye(P, dtype=np.float32),
        "c_onehot": onehot,
        "c_turn": turn,
        "c_strip": strip,
        "c_late": np.where(late, np.float32(NEG), np.float32(0.0)).astype(np.float32),
    }


def layer(nc, a, out):
    ctx = ExitStack()
    KB = 1024
    base = -(-nc.sbuf_base // 32) * 32

    def at(name, shape, kb, dt=F32):
        return nc.alloc_sbuf_tensor_at(name, shape, dt, offset=base + int(kb * KB))

    def sem(name):
        return ctx.enter_context(nc.semaphore(name))

    with ctx:
        raw = [at(f"raw{i}", [P, KD, SW], 8 * i) for i in range(2)]
        wh = [at(f"weight_high{i}", [P, KD, SW], 16 + 8 * i, F32R) for i in range(2)]
        wl = [at(f"weight_low{i}", [P, KD, SW], 32 + 8 * i, F32R) for i in range(2)]
        hTH = at("hidden_high", [P, KD, T], 48, F32R)
        hTL = at("hidden_low", [P, KD, T], 64, F32R)
        oTH = at("branch_out_high", [P, KD, T], 80, F32R)
        oTL = at("branch_out_low", [P, KD, T], 96, F32R)
        merged = at("merged", [P, KD, T], 112)
        qT = at("qT", [P, 2, T], 128)
        kT = at("kT", [P, 2, T], 132)
        vN = at("vN", [P, NT, 2 * P], 136)
        probs = at("probs", [P, 4, UNIT], 140)
        probsT = at("probsT", [P, 3, T], 160)
        xN = at("x_rows", [P, NT, D], 96)
        latN = at("latent_rows", [P, NT, 704], 80)
        latH = at("latent_high", [P, 5, T], 170, F32R)
        latL = at("latent_low", [P, 5, T], 180, F32R)
        qrT = at("q_rope", [P, T], 190)
        krT = at("k_rope", [P, T], 192)
        cosT = at("cosT", [P, T], 194)
        sinT = at("sinT", [P, T], 196)
        ropeTmp = at("rope_tmp", [P, T], 198)
        strip0 = at("causal_strip", [P, T], 150)
        posI = at("positions_int", [P, T], 154, I32)
        angle = at("angle", [P, T], 156)
        turns = at("turns", [P, T], 158)
        iqT = at("index_q", [P, 4, T], 112)
        ikT = at("index_k", [P, T], 120)
        iscore = at("index_score", [P, UNIT - P], 152)
        relu = at("index_relu", [P, 2, T], 200)
        selb = at("selection_bias", [P, UNIT - P], 200)
        strips = at("bias_strips", [P, 2, 2, T], 170)
        biased = at("selection_strips", [P, 2, UNIT], 178)
        kcT = at("kcT", [P, 2, T], 128)
        vcT = at("vcT", [P, 2, T], 132)
        flat_ = at("flat", [P, 2, 32, NC], 136)
        FLAT = 32 * 2 * NC
        flatH = [at(f"flat_high{kv}", [P, FLAT + P - 2 * NC], 144 + 16.25 * kv, F32R) for kv in range(2)]
        flatL = [at(f"flat_low{kv}", [P, FLAT + P - 2 * NC], 152.125 + 16.25 * kv, F32R) for kv in range(2)]
        hidR = at("cmp_hidden_rows", [2 * NC, 2, SW], 194)
        hid = at("cmp_hidden", [P, 2, 2, 2 * NC], 188)
        cmpW2 = at("cmp_w2", [P, 2, 2, P], 189)
        kcmpT = at("k_cmpT", [P, 2 * NC], 191)
        vcmp = at("v_cmp", [32, 2, P], 191.25)
        late = at("cmp_mask", [P, NT, NC], 192.25)
        probC = at("cmp_probs", [P, 2, NT, 32], 192.75)
        gateN = at("nsa_gates", [P, NT, 24], 197.75)
        sig = at("branch_gate", [P, 2, T], 128)
        gated = at("gated", [P, 2, T], 132)
        mgH = at("merged_high", [P, KD, T], 140, F32R)
        mgL = at("merged_low", [P, KD, T], 156, F32R)
        yT = at("y", [P, KD, T], 172)
        square = at("square", [P, 2, 2, T], 188)
        rstd = at("rstd", [P, T], 196)
        XT = at("residual", [P, KD, T], 80)
        xN2 = at("x_rows_again", [P, NT, D], 186)
        memN = at("mem_rows", [P, 2, D], 64)
        memH = at("mem_high", [P, KD, MEM], 96, F32R)
        memL = at("mem_low", [P, KD, MEM], 104, F32R)
        normed = at("normed", [P, 2, T], 201.5)
        kxT = at("cross_k", [P, KD, MEM], 112)
        vxN = at("cross_v", [P, 2, D], 120)
        probX = at("cross_probs", [P, NT, MEM], 132)
        probXT = at("cross_probsT", [P, 2, T], 136)
        coH = at("cross_out_high", [P, KD, T], 140, F32R)
        coL = at("cross_out_low", [P, KD, T], 156, F32R)
        h1H = at("up_high", [P, 16, T], 96, F32R)
        h1L = at("up_low", [P, 16, T], 128, F32R)
        h1 = at("up", [P, 2, 2, T], 160)
        outN = at("out_rows", [P, NT, D], 128)
        ident = at("ident", [P, P], 206)
        small = at("small", [P, 288], 206.5)
        gains = small[:, 0:61]
        posT = small[:, 61:125]
        stat = small[:, 125:133]
        rstat = small[:, 133:141]
        rowmax = small[:, 141:157]
        negmax = small[:, 157:173]
        total = small[:, 173:189]
        rtotal = small[:, 189:205]
        turn = small[:, 205:207]
        top8 = small[:, 207:215]
        maxC = small[:, 215:223]
        totC = small[:, 223:231]
        rC = small[:, 231:239]
        iw = small[:, 239:271].rearrange("p (t h) -> p t h", h=8)
        nstat = small[:, 271:279]
        gainRows = at("gain_rows", [64, P], 128)
        posRows = at("pos_rows", [64, P], 128.5)
        tab = at("bias_table", [32, 16], 129)
        onehot = at("onehot", [32, T], 130)
        biasRow = at("bias_row", [16, T + P], 132)
        ones = at("ones", [P, P], 205.5)

        def ps(name, shape):
            return ctx.enter_context(nc.psum_tensor(name, shape, F32))

        G = [ps("dense0", [P, 2, T]), ps("dense1", [P, 2, T])]
        S = [ps("score0", [P, T]), ps("score1", [P, T])]
        PT = ps("turned", [P, T])
        OT = ps("attended", [P, T])

        def flat(tile):
            return tile[:, :, :].rearrange("p k c -> p (k c)")

        def wide(tile, k, c):
            return flat(tile)[:, 0:k * c].rearrange("p (k c) -> p k c", c=c)

        win = a["w_in"][0].rearrange("(k p) c -> p k c", p=P)

        def square_slab(w, c0, c1, k0=0):
            return [(w[:, k0:k0 + KD, c0:c1], lambda t: t[:, :, 0:c1 - c0])]

        def rows(name, *i):
            w = a[name][0]
            for j in i:
                w = w[j]
            return w.rearrange("(k p) c -> p k c", p=P)

        slabs, slab_at = [], {}

        def slab(name, pieces):
            slab_at[name] = len(slabs)
            slabs.append(pieces)

        slab(("lat", 0), square_slab(win, 0, 256))
        slab(("lat", 1), square_slab(win, 256, 512))
        slab(("lat", 2), square_slab(win, 512, 704))
        slab(("kr",), square_slab(win, C_LAT + DQ + DKV, C_LAT + DQ + DKV + ROPE))
        slab(("iq", 0), square_slab(win, C_IQ, C_IQ + 256))
        slab(("iq", 1), square_slab(win, C_IQ + 256, C_IQ + 512))
        slab(("ik",), square_slab(win, C_IK, C_IK + 72))
        for p in range(4):
            slab(("uq", p), [(rows("mla_w_uq")[:, :, p * 384:(p + 1) * 384], lambda t: wide(t, 3, 384))])
            slab(("ukv", p), [(rows("mla_w_ukv")[:, :, p * 512:(p + 1) * 512], lambda t: wide(t, 2, 512))])

        def merge_slabs(b):
            for n in range(GROUPS):
                slab(("bg", b, n), square_slab(win, C_BG + b * D + n * SW, C_BG + b * D + (n + 1) * SW))
                slab(("bp", b, n), square_slab(rows("w_branch", b), n * SW, (n + 1) * SW))

        merge_slabs(0)
        for p in range(4):
            for name, c in (("dq", C_DQ), ("dk", C_DK), ("dv", C_DV)):
                slab((name, p), square_slab(win, c + p * SW, c + (p + 1) * SW))
        merge_slabs(1)
        slab(("kc",), square_slab(win, C_KC, C_KC + SW))
        slab(("vc",), square_slab(win, C_VC, C_VC + SW))
        slab(("ng",), square_slab(win, C_NG, C_NG + 24))
        for kv in range(2):
            for c in range(4):
                slab(("cw", kv, c), square_slab(rows("nsa_cmp_w1", kv), 0, SW, c * KD))
        for p in range(4):
            g = p // 2
            slab(("nq", p), square_slab(win, C_NQ + p * SW, C_NQ + (p + 1) * SW))
            if p % 2 == 0:
                for name, c0, c1 in (("kk", C_KS, C_KW), ("vv", C_VS, C_VW)):
                    slab((name, g), [
                        (win[:, :, c0 + g * P:c0 + (g + 1) * P], lambda t: t[:, :, 0:P]),
                        (win[:, :, c1 + g * P:c1 + (g + 1) * P], lambda t: t[:, :, P:2 * P])])
        merge_slabs(2)
        for n in range(GROUPS):
            slab(("wo", n), square_slab(rows("w_out"), n * SW, (n + 1) * SW))
        for n in range(GROUPS):
            slab(("ck", n), square_slab(rows("cross_wkv"), n * SW, (n + 1) * SW))
        for n in range(GROUPS):
            slab(("cv", n), square_slab(rows("cross_wkv"), D + n * SW, D + (n + 1) * SW))
        for n in range(GROUPS):
            slab(("cq", n), square_slab(rows("cross_wq"), n * SW, (n + 1) * SW))
        for n in range(GROUPS):
            slab(("co", n), square_slab(rows("cross_wo"), n * SW, (n + 1) * SW))
        for f in range(2):
            for n in range(8):
                c = f * 2048 + n * SW
                slab(("up", f, n), square_slab(rows("mlp_w1"), c, c + SW))
            for n in range(GROUPS):
                for k in range(2):
                    slab(("down", f, n, k), square_slab(rows("mlp_w2"), n * SW, (n + 1) * SW, f * 16 + k * KD))
        SLABS = len(slabs)
        landed, counts = [], [0, 0]
        for s, pieces in enumerate(slabs):
            counts[s % 2] += 16 * len(pieces)
            landed.append(counts[s % 2])

        def split_pieces(s, dst, src):
            def doubled(c, n, c0, width=128):
                return [(dst[:, :, c + h * 64:c + h * 64 + n], src[:, :, c0:c0 + n]) for h in range(width // 64)]
            if s == slab_at["lat", 2]:
                return [(dst[:, :, 0:128], src[:, :, 0:128])] + doubled(128, 64, 128)
            if s == slab_at["kr",]:
                return doubled(0, 32, 32) + doubled(32, 32, 0)
            if slab_at["uq", 0] <= s < slab_at["uq", 0] + 8 and (s - slab_at["uq", 0]) % 2 == 0:
                d = wide(dst, 3, 512).rearrange("p k (q h c) -> p k q h c", q=2, h=2, c=128)[:, :, 0]
                e = wide(dst, 3, 512)[:, :, 256:512].rearrange("p k (q h c) -> p k q h c", q=2, h=2)
                r = wide(src, 3, 384).rearrange("p k (h c) -> p k h c", c=192)
                return [(d, r[:, :, :, 0:128]), (e[:, :, 0], r[:, :, :, 128:192]),
                        (e[:, :, 1, :, 0:32], r[:, :, :, 160:192]), (e[:, :, 1, :, 32:64], r[:, :, :, 128:160])]
            if slab_at["ukv", 0] <= s < slab_at["ukv", 0] + 8 and (s - slab_at["ukv", 0]) % 2 == 0:
                return [(wide(dst, 2, 512), wide(src, 2, 512))]
            if s == slab_at["ik",]:
                return doubled(0, 64, 0) + [(dst[:, :, 128:136], src[:, :, 64:72])]
            if s == slab_at["ng",]:
                return [(dst[:, :, 0:24], src[:, :, 0:24])]
            return [(dst[:, :, :], src[:, :, :])]

        product_at, takers, ready_at, used_at = {}, [], {}, {}
        events = [0]

        def part(s):
            events[0] += 1
            used_at[s] = events[0]

        def product(name, taker, s=None):
            product_at[name] = len(takers)
            takers.append(taker)
            part(s)
            ready_at[name] = events[0]

        product("setup", "V")
        for i in range(4):
            product(("x", i), "V")
        for i in range(3):
            product(("lat", i), "A", slab_at["lat", i])
        product("krope", "V", slab_at["lat", 2])
        used_at[slab_at["kr",]] = ready_at["krope"]
        product(("iq", 0), "A", slab_at["iq", 0])
        product(("iq", 1), "V", slab_at["iq", 1])
        product("ik", "V", slab_at["ik",])
        for i in range(3):
            product(("latT", i), "V")
        for p in range(4):
            product(("m1", p), "A", slab_at["uq", p])
            product(("m2", p), "V", slab_at["uq", p])
            product(("m3", p), "A", slab_at["ukv", p])
            product(("m4", p), "A", slab_at["ukv", p])

        def merge_products(b):
            for n in range(GROUPS):
                product(("bg", b, n), "A", slab_at["bg", b, n])
                product(("bp", b, n), "V", slab_at["bp", b, n])

        merge_products(0)
        for p in range(4):
            product(("dq", p), "A", slab_at["dq", p])
            product(("dk", p), "V", slab_at["dk", p])
            product(("dv", p), "A", slab_at["dv", p])
        merge_products(1)
        product("kc", "A", slab_at["kc",])
        product("vc", "A", slab_at["vc",])
        product("ng", "A", slab_at["ng",])
        for kv in range(2):
            for c in range(3):
                part(slab_at["cw", kv, c])
            product(("hid", kv), "A", slab_at["cw", kv, 3])
        for p in range(4):
            product(("nq", p), "A", slab_at["nq", p])
            if p == 0:
                product("hidT", "V")
            if p % 2 == 0:
                product(("kk", p // 2), "V", slab_at["kk", p // 2])
                if p == 0:
                    product("cmp", "V")
                product(("vv", p // 2), "A", slab_at["vv", p // 2])
        merge_products(2)
        for i in range(4):
            product(("xt", i), "A")
        for n in range(GROUPS):
            if n == 2:
                for i in range(2):
                    product(("mem", i), "V")
            product(("wo", n), "A", slab_at["wo", n])
        for n in range(GROUPS):
            product(("ck", n), "V", slab_at["ck", n])
        for n in range(GROUPS):
            product(("cv", n), "A", slab_at["cv", n])
        for n in range(GROUPS):
            product(("cq", n), "A", slab_at["cq", n])
        for n in range(GROUPS):
            product(("co", n), "A", slab_at["co", n])
        for f in range(2):
            for n in range(8):
                product(("up", f, n), "A", slab_at["up", f, n])
            for n in range(GROUPS):
                part(slab_at["down", f, n, 0])
                product(("down", f, n), "A" if f == 0 else "V", slab_at["down", f, n, 1])
        for i in range(4):
            product(("out", i), "A")
        taken_count = [takers[:i + 1].count(t) for i, t in enumerate(takers)]

        UNITS_MLA, UNITS_DSA = 8, 16
        NSA_TILES = 4 * NT + 2
        TILE_NSA = UNITS_DSA * NT
        TILES = TILE_NSA + 4 * NSA_TILES
        INDEX_TILES = 3 * 8

        s_setup = sem("setup_loaded")
        s_x = [sem(f"x_loaded{t}") for t in range(NT)]
        s_pos = sem("positions_loaded")
        s_strip0 = sem("causal_strip_loaded")
        loaded = [sem("slab_loaded0"), sem("slab_loaded1")]
        high_ready = sem("slab_high_ready")
        low_ready = sem("slab_low_ready")
        product_ready = sem("product_ready")
        taken = {"A": sem("product_taken_by_act"), "V": sem("product_taken_by_dve")}
        act_step = sem("act_step")
        dve_step = sem("dve_step")
        pool_step = sem("pool_step")
        x_scaled = sem("x_rows_scaled")
        xsum_ready = sem("x_square_sums")
        xroot_ready = sem("x_root_arg")
        root_done = sem("root_done")
        hidden_high = sem("hidden_high_ready")
        bias_row_ready = sem("bias_row_ready")
        scratch_written = sem("scratch_written")
        angle_ready = sem("angle_ready")
        sine_ready = sem("sine_ready")
        latsum_ready = sem("latent_square_sums")
        lat_scaled = sem("latent_scaled")
        lat_high = sem("latent_high_ready")
        index_ready = sem("index_scores_ready")
        index_taken = sem("index_scores_taken")
        index_added = sem("index_scores_added")
        selection_ready = sem("selection_ready")
        score_ready = sem("scores_ready")
        score_taken = sem("scores_taken")
        negmax_ready = sem("negmax_ready")
        exp_done = sem("exp_done")
        probs_ready = sem("probs_ready")
        turned_ready = sem("turned_ready")
        probsT_ready = sem("probsT_ready")
        attended_ready = sem("attended_ready")
        attended_high = sem("attended_high")
        attended_taken = sem("attended_taken")
        merge_added = sem("merge_added")
        strips_loaded = [sem("strips_loaded0"), sem("strips_loaded1")]
        biased_ready = sem("biased_ready")
        flat_ready = sem("flat_ready")
        flat_high = sem("flat_high_ready")
        flat_split = sem("flat_split")
        cmp2_loaded = sem("cmp_w2_loaded")
        cmpmax_ready = sem("cmp_max_ready")
        cmpexp_done = sem("cmp_exp_done")
        merged_high = sem("merged_high_ready")
        merged_ready = sem("merged_ready")
        x2_loaded = sem("x_loaded_again")
        mem_loaded = sem("mem_loaded")
        memsum_ready = sem("mem_square_sums")
        memroot_ready = sem("mem_root_arg")
        mem_scaled = sem("mem_scaled")
        mem_high = sem("mem_high_ready")
        post_sum = [sem(f"post_sum{j}") for j in range(3)]
        post_arg = [sem(f"post_root_arg{j}") for j in range(3)]
        post_scaled = [sem(f"post_scaled{j}") for j in range(3)]
        resid_ready = [sem(f"residual_ready{j}") for j in range(3)]
        resid_dve = [sem(f"residual_ready_dve{j}") for j in range(3)]
        presq_ready = [sem(f"pre_squares{j}") for j in range(2)]
        presum = [sem(f"pre_sum{j}") for j in range(2)]
        pre_arg = [sem(f"pre_root_arg{j}") for j in range(2)]
        normed_ready = [sem(f"normed_ready{j}") for j in range(2)]
        nhigh_ready = [sem(f"normed_high{j}") for j in range(2)]
        nhid_ready = [sem(f"normed_split{j}") for j in range(2)]
        cross_ready = sem("cross_scores_ready")
        cross_taken = sem("cross_scores_taken")
        cmax_ready = sem("cross_max_ready")
        cexp_done = sem("cross_exp_done")
        crt_ready = sem("cross_rtotal_ready")
        cprobs_ready = sem("cross_probs_ready")
        cturned_ready = sem("cross_turned_ready")
        cprobsT_ready = sem("cross_probsT_ready")
        catt_ready = sem("cross_attended_ready")
        catt_high = sem("cross_attended_high")
        catt_taken = sem("cross_attended_taken")
        up_relu = sem("up_relu")
        up_squared = sem("up_squared")
        up_high = sem("up_high_ready")
        up_ready = sem("up_ready")
        downsq_ready = sem("down_squares")
        out_written = sem("out_written")

        scratch = nc.dram_tensor("bias_scratch", (16, P, T + P), F32, kind="Internal").ap()
        block = ctx.enter_context(nc.Block())

        def out_row(w):
            return w[0].rearrange("(t p) d -> p t d", p=P)

        @block.sync
        def _(sp):
            sp.dma_start(turn, a["c_turn"]).then_inc(s_pos, 16)
            sp.dma_start(posI[:, :], a["positions"][0].partition_broadcast(P)).then_inc(s_pos, 16)
            for t in range(NT):
                sp.dma_start(xN[:, t, :], out_row(a["x"])[:, t, :]).then_inc(s_x[t], 16)
            sp.dma_start(ident[:, :], a["c_ident"]).then_inc(s_setup, 16)
            sp.dma_start(gainRows[0:56, :], a["norm_gains"][0].rearrange("n (k p) -> (n k) p", p=P)).then_inc(s_setup, 16)
            sp.dma_start(gainRows[56:59, :], a["mla_q_norm"][0].rearrange("(k p) -> k p", p=P)).then_inc(s_setup, 16)
            sp.dma_start(gainRows[59:61, :], a["mla_kv_norm"][0].rearrange("(k p) -> k p", p=P)).then_inc(s_setup, 16)
            sp.dma_start(posRows[:, :], a["nsa_cmp_pos"][0].rearrange("n l d -> (n l) d")).then_inc(s_setup, 16)
            sp.dma_start(tab[:, :], a["rel_bias"]).then_inc(s_setup, 16)
            sp.dma_start(onehot[:, :], a["c_onehot"]).then_inc(s_setup, 16)
            sp.dma_start(strip0[:, :], a["c_strip"]).then_inc(s_strip0, 16)

            def load(s):
                if s >= 2:
                    sp.wait_ge(low_ready, s - 1)
                for src, view in slabs[s]:
                    sp.dma_start(view(raw[s % 2]), src).then_inc(loaded[s % 2], 16)

            for s in range(slab_at["cw", 0, 0]):
                load(s)
            sp.wait_ge(attended_taken, 16)
            sp.dma_start(cmpW2[:, :, :, :].rearrange("p n k d -> p (n k) d"),
                         a["nsa_cmp_w2"][0].rearrange("n (k p) d -> p (n k) d", p=P)).then_inc(cmp2_loaded, 16)
            sp.dma_start(late[:, :, :], a["c_late"]).then_inc(cmp2_loaded, 16)
            for s in range(slab_at["cw", 0, 0], slab_at["bp", 2, 1]):
                load(s)
            sp.wait_ge(attended_taken, 24)
            sp.dma_start(xN2[:, :, :], out_row(a["x"])).then_inc(x2_loaded, 16)
            for s in range(slab_at["bp", 2, 1], slab_at["wo", 2]):
                load(s)
            sp.wait_ge(product_ready, ready_at["bp", 2, GROUPS - 1])
            sp.dma_start(memN[:, :, :], out_row(a["mem"])).then_inc(mem_loaded, 16)
            for s in range(slab_at["wo", 2], SLABS):
                load(s)
            for i in range(NT):
                sp.wait_ge(taken["A"], taken_count[product_at["out", i]])
                sp.dma_start(out_row(out)[:, :, i * SW:(i + 1) * SW], outN[:, :, i * SW:(i + 1) * SW]).then_inc(out_written, 16)
            sp.wait_ge(out_written, 16 * NT)

        @block.tensor
        def _(pe):
            def free(g):
                if g >= 2:
                    pe.wait_ge(taken[takers[g - 2]], taken_count[g - 2])

            def blocks3(out_ap, wide_pair, move_pair, first, last):
                (ah, al), (bh, bl) = wide_pair, move_pair
                pe.matmul(out_ap, ah, bh, start=first, stop=False)
                pe.matmul(out_ap, ah, bl, start=False, stop=False)
                return pe.matmul(out_ap, al, bh, start=False, stop=last)

            def t_mode(s, dst, cols, chunks, act, wait_chunk=None, k0=0, k_all=None, w0=0):
                high, low = wh[s % 2], wl[s % 2]
                k_all = k_all or chunks
                pe.wait_ge(low_ready, s + 1)
                for k in range(chunks):
                    if wait_chunk:
                        wait_chunk(k)
                    for b, c in enumerate(cols):
                        mm = blocks3(dst[b], (c(high, w0 + k), c(low, w0 + k)), (act[0][:, k0 + k, :], act[1][:, k0 + k, :]),
                                     k0 + k == 0, k0 + k == k_all - 1)
                return mm

            def n_mode(s, dst, cols, chunks, act, tiles=NT, k0=0):
                high, low = wh[s % 2], wl[s % 2]
                pe.wait_ge(low_ready, s + 1)
                for t in range(tiles):
                    for k in range(chunks):
                        mm = blocks3(dst(t), (act[0][:, k0 + k, t * P:(t + 1) * P], act[1][:, k0 + k, t * P:(t + 1) * P]),
                                     (cols(high, k), cols(low, k)), k == 0, k == chunks - 1)
                return mm

            def two(g):
                return [G[g % 2][:, 0, :], G[g % 2][:, 1, :]]

            def pair_cols(c0=0, c1=P):
                return [lambda t, k: t[:, k, c0:c0 + P], lambda t, k: t[:, k, c1:c1 + P]]

            def tokens_out(g):
                v = G[g % 2][:, :, :].rearrange("p b (t c) -> p (b t) c", c=SW)
                return lambda t: v[:, t, :]

            hT = (hTH, hTL)
            both = pair_cols()

            def all_cols(t, k):
                return t[:, k, :]

            g = product_at["setup"]
            pe.wait_ge(s_setup, 7 * 16)
            pe.transpose(G[0][:, 0, 0:61], gainRows[0:61, :], ident[0:61, 0:61])
            pe.transpose(G[0][:, 0, 64:128], posRows[:, :], ident[0:64, 0:64])
            pe.matmul(G[0][0:16, 1, :], tab[:, :], onehot[:, :], start=True, stop=True).then_inc(product_ready, 1)
            for i in range(4):
                g = product_at["x", i]
                free(g)
                for b in range(2):
                    for t in range(NT):
                        pe.wait_ge(x_scaled, t + 1)
                        mm = pe.transpose(G[g % 2][:, b, t * P:(t + 1) * P], xN[:, t, (2 * i + b) * P:(2 * i + b + 1) * P], ident[:, :])
                mm.then_inc(product_ready, 1)
            pe.wait_ge(taken["V"], taken_count[product_at["x", 3]])
            for i in range(2):
                g, s = product_at["lat", i], slab_at["lat", i]
                free(g)
                n_mode(s, tokens_out(g), all_cols, KD, hT).then_inc(product_ready, 1)
            g, s = product_at["lat", 2], slab_at["lat", 2]
            free(g)
            v = G[g % 2][:, 0, :].rearrange("p (t c) -> p t c", c=P)
            n_mode(s, lambda t: v[:, t, :], lambda t, k: t[:, k, 0:P], KD, hT).then_inc(product_ready, 1)
            g = product_at["krope"]
            free(g)

            t_mode(s, two(g)[0:1], pair_cols(P)[0:1], KD, hT)
            t_mode(slab_at["kr",], two(g)[1:2], pair_cols(0)[0:1], KD, hT).then_inc(product_ready, 1)
            for i in range(2):
                g = product_at["iq", i]
                free(g)
                t_mode(slab_at["iq", i], two(g), both, KD, hT).then_inc(product_ready, 1)
            g, s = product_at["ik"], slab_at["ik",]
            free(g)
            t_mode(s, two(g)[0:1], pair_cols(0)[0:1], KD, hT)
            n_mode(s, lambda t: G[g % 2][:, 1, t * 8:(t + 1) * 8], lambda t, k: t[:, k, 128:136], KD, hT).then_inc(product_ready, 1)
            pe.wait_ge(lat_scaled, NT)
            for i in range(3):
                g = product_at["latT", i]
                free(g)
                for b in range(2 if i < 2 else 1):
                    for t in range(NT):
                        c = (2 * i + b) * P
                        mm = pe.transpose(G[g % 2][:, b, t * P:(t + 1) * P], latN[:, t, c:c + P], ident[:, :])
                mm.then_inc(product_ready, 1)
            pe.wait_ge(taken["A"], taken_count[product_at["iq", 0]])
            pe.wait_ge(taken["V"], taken_count[product_at["ik"]])
            n = 0
            for i in range(1, NT):
                for h in range(8):
                    if n >= 2:
                        pe.wait_ge(index_taken, n - 1)
                    r = slice(64 * (h % 2), 64 * (h % 2) + 64)
                    pe.matmul(S[n % 2][:, 0:(i + 1) * P], iqT[r, h // 2, i * P:(i + 1) * P],
                              ikT[r, 0:(i + 1) * P], start=True, stop=True).then_inc(index_ready, 1)
                    n += 1
            pe.wait_ge(index_taken, INDEX_TILES)

            def score_tile(n, terms, cols):
                if n >= 2:
                    pe.wait_ge(score_taken, n - 1)
                for j, (q, k) in enumerate(terms):
                    mm = pe.matmul(S[n % 2][:, 0:cols], q, k, start=j == 0, stop=j == len(terms) - 1)
                mm.then_inc(score_ready, 1)

            def attend(heads, m):
                def turn_tile(unit, probs_of, i0, rows, m):
                    pe.wait_ge(probs_ready, unit + 1)
                    if m:
                        pe.wait_ge(probsT_ready, m)
                    for i in range(i0, NT):
                        mm = pe.transpose(PT[0:rows, (i - i0) * P:(i - i0 + 1) * P], probs_of(i), ident[:, :])
                    mm.then_inc(turned_ready, 1)

                def value_tile(att, first, last, value, i0, rows, m):
                    pe.wait_ge(probsT_ready, m + 1)
                    if first and att:
                        pe.wait_ge(attended_taken, att)
                    mm = pe.matmul(OT[:, i0 * P:T], value, probsT[0:rows, m % 3, 0:T - i0 * P],
                                   start=first, stop=last)
                    if last:
                        mm.then_inc(attended_ready, 1)

                late_one = None
                for att, parts in heads:
                    for n, (unit, probs_of, i0, rows, value) in enumerate(parts):
                        turn_tile(unit, probs_of, i0, rows, m)
                        if late_one:
                            value_tile(*late_one)
                        late_one = (att, n == 0, n == len(parts) - 1, value, i0, rows, m)
                        m += 1
                value_tile(*late_one)

            def causal_parts(unit, slot, value_of):
                def block(j):
                    return lambda i: probs[:, slot, TRI[i] + j * P:TRI[i] + (j + 1) * P]
                return [(unit, block(j), j, P, value_of(j)) for j in range(NT)]

            lat = (latH, latL)

            def uq_cols(c):
                return lambda t, k: wide(t, 3, 512)[:, k, c:c + P]

            def mla_values(p):
                attend([(2 * p + h, causal_parts(2 * p + h, h, lambda j, h=h: vN[:, j, h * P:(h + 1) * P]))
                        for h in range(2)], 8 * p)

            def mla_v(p):
                s = slab_at["ukv", p]
                g = product_at["m4", p]
                free(g)
                v = G[g % 2][:, :, :].rearrange("p b (t h c) -> p (b t) h c", h=2, c=P)
                n_mode(s, lambda t: v[:, t, :, :],
                       lambda t, k: wide(t, 2, 512)[:, k, :].rearrange("p (h c) -> p h c", c=256)[:, :, P:2 * P],
                       2, (latH[:, 3:5, :], latL[:, 3:5, :])).then_inc(product_ready, 1)

            for p in range(4):
                s = slab_at["uq", p]
                g = product_at["m1", p]
                free(g)
                if p == 0:
                    pe.wait_ge(taken["V"], taken_count[product_at["latT", 2]])
                t_mode(s, two(g), [uq_cols(0), uq_cols(128)], 3, lat).then_inc(product_ready, 1)
                g = product_at["m2", p]
                free(g)
                t_mode(s, two(g), [uq_cols(256), uq_cols(384)], 3, lat).then_inc(product_ready, 1)
                s = slab_at["ukv", p]
                g = product_at["m3", p]
                free(g)
                t_mode(s, two(g), [lambda t, k: wide(t, 2, 512)[:, k, 0:P], lambda t, k: wide(t, 2, 512)[:, k, 256:384]],
                       2, (latH[:, 3:5, :], latL[:, 3:5, :])).then_inc(product_ready, 1)
                if p:
                    mla_values(p - 1)
                else:
                    mla_v(p)
                pe.wait_ge(taken["V"], taken_count[product_at["m2", p]])
                pe.wait_ge(taken["A"], taken_count[product_at["m3", p]])
                for h in range(2):
                    r = slice(64 * h, 64 * h + 64)
                    for i in range(NT):
                        q = slice(i * P, (i + 1) * P)
                        score_tile((2 * p + h) * NT + i, [(qT[:, h, q], kT[:, h, 0:(i + 1) * P]),
                                                          (qrT[r, q], krT[r, 0:(i + 1) * P])], (i + 1) * P)
                if p:
                    mla_v(p)
            pe.wait_ge(taken["A"], taken_count[product_at["m4", 3]])

            def merge(b, last_values):
                for n in range(GROUPS):
                    g = product_at["bg", b, n]
                    free(g)
                    t_mode(slab_at["bg", b, n], two(g), both, KD, hT).then_inc(product_ready, 1)
                    if n == 0:
                        last_values()
                    g = product_at["bp", b, n]
                    free(g)
                    pe.wait_ge(attended_taken, 8 * (b + 1))
                    t_mode(slab_at["bp", b, n], two(g), both, KD, (oTH, oTL)).then_inc(product_ready, 1)

            merge(0, lambda: mla_values(3))

            def dsa_values(p):
                attend([(8 + 2 * p + h, causal_parts(8 + 2 * p + h, h, lambda j, h=h: vN[:, j, h * P:(h + 1) * P]))
                        for h in range(2)], 32 + 8 * p)

            def dsa_v(p):
                g = product_at["dv", p]
                free(g)
                n_mode(slab_at["dv", p], tokens_out(g), all_cols, KD, hT).then_inc(product_ready, 1)

            for p in range(4):
                for name in ("dq", "dk"):
                    g = product_at[name, p]
                    free(g)
                    t_mode(slab_at[name, p], two(g), both, KD, hT).then_inc(product_ready, 1)
                if p:
                    dsa_values(p - 1)
                else:
                    dsa_v(0)
                pe.wait_ge(taken["A"], taken_count[product_at["dq", p]])
                pe.wait_ge(taken["V"], taken_count[product_at["dk", p]])
                for h in range(2):
                    for i in range(NT):
                        score_tile((8 + 2 * p + h) * NT + i, [(qT[:, h, i * P:(i + 1) * P], kT[:, h, 0:(i + 1) * P])], (i + 1) * P)
                if p:
                    dsa_v(p)
            pe.wait_ge(taken["A"], taken_count[product_at["dv", 3]])
            merge(1, lambda: dsa_values(3))

            for name in ("kc", "vc"):
                g = product_at[name]
                free(g)
                t_mode(slab_at[name,], two(g), both, KD, hT).then_inc(product_ready, 1)
            g = product_at["ng"]
            free(g)
            n_mode(slab_at["ng",], lambda t: G[g % 2][:, 0, t * 24:(t + 1) * 24], lambda t, k: t[:, k, 0:24], KD, hT).then_inc(product_ready, 1)
            for kv in range(2):
                g = product_at["hid", kv]
                free(g)
                pe.wait_ge(flat_split, kv + 1)
                for c in range(4):
                    s = slab_at["cw", kv, c]
                    pe.wait_ge(low_ready, s + 1)
                    for k in range(KD):
                        l = (c * KD + k) * 2 * NC
                        mm = blocks3(G[g % 2][:, 0, 0:SW], (flatH[kv][:, l:l + P], flatL[kv][:, l:l + P]),
                                     (wh[s % 2][:, k, :], wl[s % 2][:, k, :]), c + k == 0, c == 3 and k == KD - 1)
                    mm.then_inc(product_ready, 1)

            def turn_hidden():
                g = product_at["hidT"]
                free(g)
                pe.wait_ge(taken["A"], taken_count[product_at["hid", 1]])
                for kv in range(2):
                    for k in range(2):
                        col = (2 * kv + k) * 2 * NC
                        mm = pe.transpose(G[g % 2][:, 0, col:col + 2 * NC], hidR[:, kv, k * P:(k + 1) * P],
                                          ident[0:2 * NC, 0:2 * NC])
                mm.then_inc(product_ready, 1)

            def compress():
                g = product_at["cmp"]
                free(g)
                pe.wait_ge(cmp2_loaded, 32)
                pe.wait_ge(taken["V"], taken_count[product_at["hidT"]])
                for k in range(2):
                    pe.matmul(G[g % 2][:, 0, 0:2 * NC], cmpW2[:, 0, k, :], hid[:, 0, k, :], start=k == 0, stop=k == 1)
                for r in range(2):
                    for k in range(2):
                        mm = pe.matmul(G[g % 2][0:NC, 1, r * P:(r + 1) * P], hid[:, 1, k, r * NC:(r + 1) * NC], cmpW2[:, 1, k, :],
                                       start=k == 0, stop=k == 1)
                mm.then_inc(product_ready, 1)

            def nsa_values(p):
                heads = []
                for h in range(2):
                    parts = []
                    for w in range(2):
                        parts += causal_parts(16 + 6 * p + 2 * h + w, 2 * h + w, lambda j, w=w: vN[:, j, w * P:(w + 1) * P])
                    parts.append((16 + 6 * p + 4 + h, lambda i, h=h: probC[:, h, i, 0:NC], 0, NC, vcmp[0:NC, p // 2, :]))
                    heads.append((16 + 2 * p + h, parts))
                attend(heads, 64 + 18 * p)

            for p in range(4):
                r = p // 2
                g = product_at["nq", p]
                free(g)
                t_mode(slab_at["nq", p], two(g), both, KD, hT).then_inc(product_ready, 1)
                if p == 0:
                    turn_hidden()
                if p % 2 == 0:
                    g = product_at["kk", r]
                    free(g)
                    t_mode(slab_at["kk", r], two(g), both, KD, hT).then_inc(product_ready, 1)
                    if p == 0:
                        compress()
                if p:
                    nsa_values(p - 1)
                if p % 2 == 0:
                    g = product_at["vv", r]
                    free(g)
                    n_mode(slab_at["vv", r], tokens_out(g), all_cols, KD, hT).then_inc(product_ready, 1)
                pe.wait_ge(taken["A"], taken_count[product_at["nq", p]])
                pe.wait_ge(taken["V"], taken_count[product_at["kk", r] if r else product_at["cmp"]])
                n = TILE_NSA + NSA_TILES * p
                for h in range(2):
                    for w in range(2):
                        for i in range(NT):
                            score_tile(n, [(qT[:, h, i * P:(i + 1) * P], kT[:, w, 0:(i + 1) * P])], (i + 1) * P)
                            n += 1
                for h in range(2):
                    if n >= 2:
                        pe.wait_ge(score_taken, n - 1)
                    for i in range(NT):
                        mm = pe.matmul(S[n % 2][:, i * 32:i * 32 + NC], qT[:, h, i * P:(i + 1) * P],
                                       kcmpT[:, r * NC:(r + 1) * NC], start=True, stop=True)
                    mm.then_inc(score_ready, 1)
                    n += 1
                if p % 2 == 0:
                    pe.wait_ge(taken["A"], taken_count[product_at["vv", r]])
            merge(2, lambda: nsa_values(3))

            pe.wait_ge(x2_loaded, 16)
            for i in range(4):
                g = product_at["xt", i]
                free(g)
                for b in range(2):
                    for t in range(NT):
                        mm = pe.transpose(G[g % 2][:, b, t * P:(t + 1) * P], xN2[:, t, (2 * i + b) * P:(2 * i + b + 1) * P], ident[:, :])
                mm.then_inc(product_ready, 1)

            def turn_memory():
                pe.wait_ge(mem_scaled, 2)
                for i in range(2):
                    g = product_at["mem", i]
                    free(g)
                    for c in range(4):
                        for t in range(2):
                            col = c % 2 * MEM + t * P
                            mm = pe.transpose(G[g % 2][:, c // 2, col:col + P], memN[:, t, (4 * i + c) * P:(4 * i + c + 1) * P], ident[:, :])
                    mm.then_inc(product_ready, 1)

            def wait_count(sem_, per=1):
                return lambda k: pe.wait_ge(sem_, k + 1)

            def post_squares(j, n, total_n=GROUPS, ready=None):
                pe.wait_ge(ready[0], ready[1])
                for b in range(2):
                    mm = pe.matmul(PT[:, :], ones[:, :], square[:, n % 2, b, :], start=n == 0 and b == 0,
                                   stop=n == total_n - 1 and b == 1)
                if n == total_n - 1:
                    mm.then_inc(post_sum[j], 1)

            def out_projection(j, name, act, wait_chunk, begun=0):
                for n in range(GROUPS):
                    if name == "wo" and n == 2:
                        turn_memory()
                    g = product_at[name, n]
                    free(g)
                    k0 = begun if n < 2 else 0
                    t_mode(slab_at[name, n], two(g), both, KD - k0, act, (lambda k: wait_chunk(k0 + k)) if n == 0 else None,
                           k0, KD, k0).then_inc(product_ready, 1)
                    if n:
                        post_squares(j, n - 1, ready=(taken["A"], taken_count[product_at[name, n - 1]]))
                post_squares(j, GROUPS - 1, ready=(taken["A"], taken_count[g]))

            def pre_squares(j):
                for c in range(KD):
                    pe.wait_ge(presq_ready[j], c + 1)
                    pe.matmul(OT[:, :], ones[:, :], square[:, c // 2 % 2, c % 2, :], start=c == 0,
                              stop=c == KD - 1).then_inc(presum[j], 1)

            out_projection(0, "wo", (mgH, mgL), lambda k: pe.wait_ge(merged_ready, k // 2 + 1))
            pe.wait_ge(taken["V"], taken_count[product_at["mem", 1]])
            mem = (memH, memL)
            for n in range(GROUPS):
                if n == 2:
                    pre_squares(0)
                g = product_at["ck", n]
                free(g)
                t_mode(slab_at["ck", n], [G[g % 2][:, b, 0:MEM] for b in range(2)], both, KD, mem).then_inc(product_ready, 1)
            for n in range(GROUPS):
                g = product_at["cv", n]
                free(g)
                n_mode(slab_at["cv", n], lambda t: G[g % 2][:, t, 0:SW], all_cols, KD, mem, tiles=2).then_inc(product_ready, 1)

            def cross_values(n):
                pe.wait_ge(cprobs_ready, n + 1)
                pe.wait_ge(cross_taken, (n + 1) * NT)
                for j in range(2):
                    if n:
                        pe.wait_ge(cprobsT_ready, 2 * n)
                    for i in range(NT):
                        mm = pe.transpose((PT, S[0])[j][:, i * P:(i + 1) * P], probX[:, i, j * P:(j + 1) * P], ident[:, :])
                    mm.then_inc(cturned_ready, 1)
                pe.wait_ge(cprobsT_ready, 2 * n + 2)
                if n:
                    pe.wait_ge(catt_taken, 2 * n)
                for b in range(2):
                    for j in range(2):
                        mm = pe.matmul((OT, S[1])[b][:, :], vxN[:, j, n * SW + b * P:n * SW + (b + 1) * P], probXT[:, j, :],
                                       start=j == 0, stop=j == 1)
                    mm.then_inc(catt_ready, 1)

            pe.wait_ge(score_taken, TILES)
            for n in range(GROUPS):
                g = product_at["cq", n]
                free(g)
                t_mode(slab_at["cq", n], two(g), both, KD, hT, wait_count(nhid_ready[0]) if n == 0 else None).then_inc(product_ready, 1)
                if n:
                    cross_values(n - 1)
                pe.wait_ge(taken["A"], taken_count[g])
                for i in range(NT):
                    m = n * NT + i
                    if i >= 2:
                        pe.wait_ge(cross_taken, m - 1)
                    if n and i == 1:
                        pe.wait_ge(catt_taken, 2 * n)
                    for b in range(2):
                        mm = pe.matmul(S[m % 2][:, 0:MEM], qT[:, b, i * P:(i + 1) * P], kxT[:, 2 * n + b, :], start=b == 0, stop=b == 1)
                    mm.then_inc(cross_ready, 1)
            for n in range(2):
                g = product_at["co", n]
                free(g)
                t_mode(slab_at["co", n], two(g), both, 6, (coH, coL), lambda k: pe.wait_ge(catt_taken, k + 1), 0, KD)
            cross_values(3)
            out_projection(1, "co", (coH, coL), lambda k: pe.wait_ge(catt_taken, k + 1), 6)
            pre_squares(1)

            up = (h1H, h1L)
            for f in range(2):
                for n in range(8):
                    g = product_at["up", f, n]
                    free(g)
                    t_mode(slab_at["up", f, n], two(g), both, KD, hT,
                           wait_count(nhid_ready[1]) if f == 0 and n == 0 else None).then_inc(product_ready, 1)
                for n in range(GROUPS):
                    g = product_at["down", f, n]
                    free(g)
                    for k in range(2):
                        t_mode(slab_at["down", f, n, k], two(g), both, KD, up,
                               lambda c, k=k: pe.wait_ge(up_ready, 8 * f + (k * KD + c) // 2 + 1), k * KD, 16).then_inc(product_ready, 1)
                    if f and n:
                        post_squares(2, n - 1, ready=(downsq_ready, n))
            post_squares(2, GROUPS - 1, ready=(downsq_ready, GROUPS))
            for i in range(4):
                g = product_at["out", i]
                free(g)
                v = tokens_out(g)
                pe.wait_ge(resid_ready[2], i + 1)
                pe.wait_ge(resid_dve[2], i + 1)
                for c in range(2):
                    for t in range(NT):
                        mm = pe.transpose(v(t)[:, c * P:(c + 1) * P], XT[:, 2 * i + c, t * P:(t + 1) * P], ident[:, :])
                mm.then_inc(product_ready, 1)

        @block.scalar
        def _(act):
            roots = [0]

            def ready(name):
                act.wait_ge(product_ready, ready_at[name])

            def copy(dst, src, scale=1.0):
                return nc.scalar.activation(dst, src, ACT.Copy, scale=scale)

            def high(s):
                if s >= SLABS:
                    return
                act.wait_ge(loaded[s % 2], landed[s])
                if s >= 2:
                    act.wait_ge(product_ready, used_at[s - 2])
                for dst, src in split_pieces(s, wh[s % 2], raw[s % 2]):
                    ins = copy(dst, src)
                ins.then_inc(high_ready, 1)

            def bank(name):
                return G[product_at[name] % 2]

            def root(tile):
                nc.scalar.activation(tile, tile, ACT.Sqrt).then_inc(root_done, 1)
                roots[0] += 1

            junk = vN[:, :, :].rearrange("p t c -> p (t c)")
            act.wait_ge(angle_ready, 1)
            nc.scalar.activation(sinT[:, :], sinT[:, :], ACT.Sin)
            nc.scalar.activation(cosT[:, :], cosT[:, :], ACT.Sin).then_inc(sine_ready, 1)

            def x_root(t):
                act.wait_ge(xroot_ready, t + 1)
                root(nstat[:, t:t + 1])

            for t in range(NT):
                act.wait_ge(s_x[t], 16)
                if t:
                    act.wait_ge(xsum_ready, t)
                nc.scalar.activation(junk, xN[:, t, :], ACT.Square, accum_out=stat[:, t:t + 1]).then_inc(xsum_ready, 1)
                if t:
                    x_root(t - 1)
            x_root(NT - 1)
            high(0)
            high(1)
            act.wait_ge(taken["V"], 1)
            for i in range(4):
                ready(("x", i))
                for b in range(2):
                    c = 2 * i + b
                    ins = copy(hTH[:, c, :], bank(("x", i))[:, b, :], gains[:, c:c + 1])
                ins.then_inc(hidden_high, 1)

            for i in range(2):
                ready(("lat", i))
                copy(latN[:, :, i * SW:(i + 1) * SW], bank(("lat", i))[:, :, :].rearrange("p b (t c) -> p (b t) c", c=SW)).then_inc(taken["A"], 1)
                high(i + 2)
            ready(("lat", 2))
            copy(latN[:, :, 512:640], bank(("lat", 2))[:, 0, :].rearrange("p (t c) -> p t c", c=P)).then_inc(taken["A"], 1)
            act.wait_ge(taken["A"], 3)
            for t in range(NT):
                if t:
                    act.wait_ge(latsum_ready, t)
                nc.scalar.activation(junk[:, 0:DQ], latN[:, t, 0:DQ], ACT.Square, accum_out=stat[:, t:t + 1])
                nc.scalar.activation(junk[:, DQ:DQ + DKV], latN[:, t, DQ:DQ + DKV], ACT.Square,
                                     accum_out=stat[:, 4 + t:5 + t]).then_inc(latsum_ready, 1)
            act.wait_ge(latsum_ready, NT + 1)
            root(nstat[:, 0:8])
            high(slab_at["lat", 2] + 2)
            high(slab_at["kr",] + 2)
            ready(("iq", 0))
            copy(iqT[:, 0:2, :], bank(("iq", 0))[:, :, :]).then_inc(taken["A"], 1)
            high(slab_at["iq", 0] + 2)
            high(slab_at["iq", 1] + 2)
            high(slab_at["ik",] + 2)
            for i in range(3):
                ready(("latT", i))
                for b in range(2 if i < 2 else 1):
                    c = 2 * i + b
                    ins = copy(latH[:, c, :], bank(("latT", i))[:, b, :], gains[:, 56 + c:57 + c])
                ins.then_inc(lat_high, 1)
            n = 0
            for i in range(1, NT):
                for h in range(8):
                    act.wait_ge(index_ready, n + 1)
                    if n >= 2:
                        act.wait_ge(index_added, n - 1)
                    nc.scalar.activation(relu[:, n % 2, 0:(i + 1) * P], S[n % 2][:, 0:(i + 1) * P], ACT.Relu).then_inc(index_taken, 1)
                    n += 1

            def exps(u, slot):
                act.wait_ge(negmax_ready, u + 1)
                for i in range(NT):
                    t = probs[:, slot, TRI[i]:TRI[i] + (i + 1) * P]
                    k = 4 * slot + i
                    ins = nc.scalar.activation(t, t, ACT.Exp, bias=negmax[:, k:k + 1], accum_out=total[:, k:k + 1])
                ins.then_inc(exp_done, 1)

            def turned(heads, m):
                def head_out(att):
                    act.wait_ge(attended_ready, att + 1)
                    copy(oTH[:, att % 8, :], OT[:, :]).then_inc(attended_high, 1)

                waiting = None
                for att, tiles in heads:
                    for n, (rows, cols) in enumerate(tiles):
                        act.wait_ge(turned_ready, m + 1)
                        copy(probsT[0:rows, m % 3, 0:cols], PT[0:rows, 0:cols]).then_inc(probsT_ready, 1)
                        m += 1
                        if n == 0 and waiting is not None:
                            head_out(waiting)
                    waiting = att
                head_out(waiting)

            causal = [(P, T - j * P) for j in range(NT)]
            if True:
                act.wait_ge(scratch_written, 16)
            for p in range(4):
                s = slab_at["uq", p]
                ready(("m1", p))
                copy(qT[:, :, :], bank(("m1", p))[:, :, :]).then_inc(taken["A"], 1)
                ready(("m2", p))
                high(s + 2)
                ready(("m3", p))
                copy(kT[:, :, :], bank(("m3", p))[:, :, :]).then_inc(taken["A"], 1)
                if p:
                    turned([(2 * (p - 1) + h, causal) for h in range(2)], 8 * (p - 1))
                for h in range(2):
                    if p:
                        exps(2 * p + h, h)
                ready(("m4", p))
                copy(vN[:, :, :], bank(("m4", p))[:, :, :].rearrange("p b (t c) -> p (b t) c", c=SW)).then_inc(taken["A"], 1)
                high(s + 3)
                for h in range(2):
                    if not p:
                        exps(2 * p + h, h)

            def merge(b, tiles, first_tile):
                for n in range(GROUPS):
                    ready(("bg", b, n))
                    if n or b:
                        last = product_at["bp", b, n - 1] if n else product_at["bp", b - 1, GROUPS - 1]
                        act.wait_ge(taken["V"], taken_count[last])
                    nc.scalar.activation(sig[:, :, :], bank(("bg", b, n))[:, :, :], ACT.Sigmoid).then_inc(taken["A"], 1)
                    high(slab_at["bg", b, n] + 2)
                    if n == 0:
                        turned([(8 * b + 6 + h, tiles) for h in range(2)], first_tile)
                    if b == 2 and n:
                        merged_split(n - 1)
                    high(slab_at["bp", b, n] + 2)
                if b == 2:
                    merged_split(GROUPS - 1)

            def merged_split(n):
                act.wait_ge(merge_added, GROUPS + n + 1)
                copy(mgH[:, 2 * n:2 * n + 2, :], merged[:, 2 * n:2 * n + 2, :]).then_inc(merged_high, 1)

            merge(0, causal, 24)
            for p in range(4):
                ready(("dq", p))
                if p == 0:
                    act.wait_ge(taken["V"], taken_count[product_at["bp", 0, GROUPS - 1]])
                copy(qT[:, :, :], bank(("dq", p))[:, :, :], HEAD_SCALE).then_inc(taken["A"], 1)
                high(slab_at["dq", p] + 2)
                high(slab_at["dk", p] + 2)
                if p:
                    turned([(8 + 2 * (p - 1) + h, causal) for h in range(2)], 32 + 8 * (p - 1))
                for h in range(2):
                    if p:
                        exps(8 + 2 * p + h, h)
                ready(("dv", p))
                copy(vN[:, :, :], bank(("dv", p))[:, :, :].rearrange("p b (t c) -> p (b t) c", c=SW)).then_inc(taken["A"], 1)
                high(slab_at["dv", p] + 2)
                for h in range(2):
                    if not p:
                        exps(8 + 2 * p + h, h)
            merge(1, causal, 56)

            act.wait_ge(taken["V"], taken_count[product_at["bp", 1, GROUPS - 1]])
            act.wait_ge(merge_added, GROUPS)
            def flat_split_high(kv):
                act.wait_ge(flat_ready, kv + 1)
                v = flatH[kv][:, 0:FLAT].rearrange("p (l c) -> p l c", c=2 * NC)
                for r in range(2):
                    ins = copy(v[:, :, r * NC:(r + 1) * NC], flat_[:, r, :, :])
                ins.then_inc(flat_high, 1)

            for kv, (name, dst) in enumerate((("kc", kcT), ("vc", vcT))):
                ready(name)
                copy(dst[:, :, :], bank(name)[:, :, :]).then_inc(taken["A"], 1)
                high(slab_at[name,] + 2)
                flat_split_high(kv)
            ready("ng")
            nc.scalar.activation(gateN[:, :, :].rearrange("p t c -> p (t c)"), bank("ng")[:, 0, 0:NT * 24], ACT.Sigmoid).then_inc(taken["A"], 1)
            high(slab_at["ng",] + 2)
            for kv in range(2):
                for c in range(4):
                    s = slab_at["cw", kv, c]
                    if c == 3:
                        ready(("hid", kv))
                        nc.scalar.activation(hidR[:, kv, :], bank(("hid", kv))[0:2 * NC, 0, 0:SW], ACT.Gelu_apprx_tanh).then_inc(taken["A"], 1)
                    high(s + 2)
            nsa = 2 * causal + [(NC, T)]
            for p in range(4):
                r = p // 2
                ready(("nq", p))
                copy(qT[:, :, :], bank(("nq", p))[:, :, :], HEAD_SCALE).then_inc(taken["A"], 1)
                high(slab_at["nq", p] + 2)
                if p % 2 == 0:
                    high(slab_at["kk", r] + 2)
                if p:
                    turned([(16 + 2 * (p - 1) + h, nsa) for h in range(2)], 64 + 18 * (p - 1))
                if p % 2 == 0:
                    ready(("vv", r))
                    copy(vN[:, :, :], bank(("vv", r))[:, :, :].rearrange("p b (t c) -> p (b t) c", c=SW)).then_inc(taken["A"], 1)
                    high(slab_at["vv", r] + 2)
                for u in range(4):
                    exps(16 + 4 * p + u, u)
                for h in range(2):
                    act.wait_ge(cmpmax_ready, 2 * p + h + 1)
                    t = probC[:, h, :, 0:NC]
                    nc.scalar.activation(t, t, ACT.Exp).then_inc(cmpexp_done, 1)
            merge(2, nsa, 64 + 54)

            for i in range(4):
                ready(("xt", i))
                copy(XT[:, 2 * i:2 * i + 2, :], bank(("xt", i))[:, :, :]).then_inc(taken["A"], 1)
            act.wait_ge(mem_loaded, 16)
            for t in range(2):
                if t:
                    act.wait_ge(memsum_ready, t)
                nc.scalar.activation(normed[:, :, :].rearrange("p b c -> p (b c)"), memN[:, t, :], ACT.Square,
                                     accum_out=stat[:, t:t + 1]).then_inc(memsum_ready, 1)
            act.wait_ge(memroot_ready, 1)
            root(nstat[:, 0:2])

            def projection(name, n):
                ready((name, n))
                g = bank((name, n))
                copy(yT[:, 2 * n:2 * n + 2, :], g[:, :, :])
                nc.scalar.activation(square[:, n % 2, :, :], g[:, :, :], ACT.Square).then_inc(taken["A"], 1)
                high(slab_at[name, n] + 2)

            def post(j):
                act.wait_ge(post_arg[j], 1)
                root(rstd[:, :])

            def pre_squared(j):
                for c in range(KD):
                    if j == 0:
                        act.wait_ge(resid_ready[j], c + 1)
                    else:
                        act.wait_ge((resid_ready, resid_dve)[c % 2][j], c // 2 + 1)
                    if c >= 4:
                        act.wait_ge(presum[j], c - 3)
                    nc.scalar.activation(square[:, c // 2 % 2, c % 2, :], XT[:, c, :], ACT.Square).then_inc(presq_ready[j], 1)

            def pre(j):
                act.wait_ge(pre_arg[j], 1)
                root(rstd[:, :])
                for c in range(KD):
                    act.wait_ge(normed_ready[j], c + 1)
                    copy(hTH[:, c, :], normed[:, c % 2, :]).then_inc(nhigh_ready[j], 1)

            for n in range(2):
                projection("wo", n)
            for i in range(2):
                ready(("mem", i))
                for c in range(4):
                    k = 4 * i + c
                    ins = copy(memH[:, k, :], bank(("mem", i))[:, c // 2, c % 2 * MEM:(c % 2 + 1) * MEM], gains[:, 24 + k:25 + k])
                ins.then_inc(mem_high, 1)
            for n in range(2, GROUPS):
                projection("wo", n)
            post(0)
            high(slab_at["ck", 0] + 2)
            pre_squared(0)
            high(slab_at["ck", 1] + 2)
            pre(0)
            for n in range(2, GROUPS):
                high(slab_at["ck", n] + 2)
            for n in range(GROUPS):
                ready(("cv", n))
                copy(vxN[:, :, n * SW:(n + 1) * SW], bank(("cv", n))[:, :, 0:SW]).then_inc(taken["A"], 1)
                high(slab_at["cv", n] + 2)

            def cross_turned(n):
                for j in range(2):
                    m = 2 * n + j
                    act.wait_ge(cturned_ready, m + 1)
                    copy(probXT[:, j, :], (PT, S[0])[j][:, :]).then_inc(cprobsT_ready, 1)
                for b in range(2):
                    act.wait_ge(catt_ready, 2 * n + b + 1)
                    copy(coH[:, 2 * n + b, :], (OT, S[1])[b][:, :]).then_inc(catt_high, 1)

            for n in range(GROUPS):
                ready(("cq", n))
                copy(qT[:, :, :], bank(("cq", n))[:, :, :], CROSS_SCALE).then_inc(taken["A"], 1)
                high(slab_at["cq", n] + 2)
                if n:
                    cross_turned(n - 1)
                for i in range(NT):
                    m = n * NT + i
                    act.wait_ge(cmax_ready, m + 1)
                    nc.scalar.activation(probX[:, i, :], S[m % 2][:, 0:MEM], ACT.Exp, bias=negmax[:, i:i + 1],
                                         accum_out=total[:, i:i + 1]).then_inc(cross_taken, 1)
            cross_turned(3)
            for n in range(GROUPS):
                projection("co", n)
            post(1)
            pre_squared(1)
            pre(1)

            def up_split(n):
                act.wait_ge(up_squared, n + 1)
                copy(h1H[:, 2 * (n % 8):2 * (n % 8) + 2, :], h1[:, n % 2, :, :]).then_inc(up_high, 1)

            for f in range(2):
                for n in range(8):
                    ready(("up", f, n))
                    u = 8 * f + n
                    if u >= 2:
                        act.wait_ge(up_ready, u - 1)
                    nc.scalar.activation(h1[:, n % 2, :, :], bank(("up", f, n))[:, :, :], ACT.Relu).then_inc(taken["A"], 1)
                    high(slab_at["up", f, n] + 2)
                    if n:
                        up_split(u - 1)
                up_split(8 * f + 7)
                for n in range(GROUPS):
                    s = slab_at["down", f, n, 0]
                    high(s + 2)
                    if f == 0:
                        ready(("down", f, n))
                        copy(yT[:, 2 * n:2 * n + 2, :], bank(("down", f, n))[:, :, :]).then_inc(taken["A"], 1)
                    else:
                        act.wait_ge(taken["V"], taken_count[product_at["down", f, n]])
                        nc.scalar.activation(square[:, n % 2, :, :], yT[:, 2 * n:2 * n + 2, :], ACT.Square).then_inc(downsq_ready, 1)
                    high(s + 3)
            post(2)
            for i in range(4):
                ready(("out", i))
                copy(outN[:, :, i * SW:(i + 1) * SW], bank(("out", i))[:, :, :].rearrange("p b (t c) -> p (b t) c", c=SW)).then_inc(taken["A"], 1)

        @block.vector
        def _(dve):
            steps = [0]
            V = nc.vector

            def link(ins):
                steps[0] += 1
                ins.then_inc(dve_step, 1)
                dve.wait_ge(dve_step, steps[0])

            def ready(name):
                dve.wait_ge(product_ready, ready_at[name])

            def bank(name):
                return G[product_at[name] % 2]

            def low(s):
                if s >= SLABS:
                    return
                dve.wait_ge(high_ready, s + 1)
                pieces = zip(split_pieces(s, wl[s % 2], raw[s % 2]), split_pieces(s, wh[s % 2], raw[s % 2]))
                for (dst, src), (hi, _) in pieces:
                    ins = V.tensor_tensor(dst, src, hi.bitcast(F32), ALU.subtract)
                ins.then_inc(low_ready, 1)

            def rest(dst, src, hi, gain):
                return V.scalar_tensor_tensor(dst, src, gain, hi.bitcast(F32), ALU.mult, ALU.subtract)

            def root_arg(dst, src, width):
                return V.tensor_scalar(dst, src, 1.0 / width, EPS, ALU.mult, ALU.add)

            dve.wait_ge(s_pos, 32)
            link(V.tensor_copy(angle[:, :], posI[:, :]))
            link(V.tensor_scalar(angle[:, :], angle[:, :], turn[:, 0:1], None, ALU.mult))
            MAGIC = 1.5 * 2.0 ** 23
            C1 = 6.28125
            C2 = 2 * np.pi - C1
            PI = 3.1415925
            for dst, quarter in ((sinT, 0.0), (cosT, 0.25)):
                link(V.tensor_scalar(turns[:, :], angle[:, :], 1 / (2 * np.pi), quarter, ALU.mult, ALU.add))
                link(V.tensor_scalar(turns[:, :], turns[:, :], MAGIC, None, ALU.add))
                link(V.tensor_scalar(turns[:, :], turns[:, :], -MAGIC, -quarter, ALU.add, ALU.add))
                link(V.scalar_tensor_tensor(dst[:, :], turns[:, :], -C1, angle[:, :], ALU.mult, ALU.add))
                link(V.scalar_tensor_tensor(dst[:, :], turns[:, :], -C2, dst[:, :], ALU.mult, ALU.add))
                ins = V.tensor_scalar(dst[:, :], dst[:, :], PI, -PI, ALU.min, ALU.max)
            ins.then_inc(angle_ready, 1)
            V.memset(biasRow[:, T:], NEG)

            def x_scale(t):
                dve.wait_ge(root_done, t + 1)
                link(V.reciprocal(rstat[:, t:t + 1], nstat[:, t:t + 1]))
                V.tensor_scalar(xN[:, t, :], xN[:, t, :], rstat[:, t:t + 1], None, ALU.mult).then_inc(x_scaled, 1)

            for t in range(NT):
                dve.wait_ge(xsum_ready, t + 1)
                root_arg(nstat[:, t:t + 1], stat[:, t:t + 1], D).then_inc(xroot_ready, 1)
                if t:
                    x_scale(t - 1)
            x_scale(NT - 1)
            dve.wait_ge(sine_ready, 1)
            link(V.tensor_scalar(sinT[:, :], sinT[:, :], turn[:, 1:2], None, ALU.mult))

            ready("setup")
            b0 = bank("setup")
            V.tensor_copy(gains, b0[:, 0, 0:61])
            V.tensor_copy(posT, b0[:, 0, 64:128])
            V.tensor_copy(biasRow[:, 0:T], b0[0:16, 1, :]).then_inc(taken["V"], 1)
            low(0)
            low(1)
            for i in range(4):
                dve.wait_ge(hidden_high, i + 1)
                for b in range(2):
                    c = 2 * i + b
                    ins = rest(hTL[:, c, :], bank(("x", i))[:, b, :], hTH[:, c, :], gains[:, c:c + 1])
                ins.then_inc(taken["V"], 1)
            def rotate(name, dst):
                ready(name)
                b = bank(name)
                V.tensor_tensor(dst[:, :], b[:, 0, :], cosT[:, :], ALU.mult)
                link(V.tensor_tensor(ropeTmp[:, :], b[:, 1, :], sinT[:, :], ALU.mult))
                V.tensor_tensor(dst[:, :], dst[:, :], ropeTmp[:, :], ALU.add).then_inc(taken["V"], 1)

            low(slab_at["lat", 0] + 2)
            low(slab_at["lat", 1] + 2)
            dve.wait_ge(latsum_ready, NT)
            root_arg(nstat[:, 0:4], stat[:, 0:4], DQ)
            root_arg(nstat[:, 4:8], stat[:, 4:8], DKV).then_inc(latsum_ready, 1)
            rotate("krope", krT)
            low(slab_at["lat", 2] + 2)
            low(slab_at["kr",] + 2)
            dve.wait_ge(root_done, 5)
            link(V.reciprocal(rstat[:, 0:8], nstat[:, 0:8]))
            for t in range(NT):
                V.tensor_scalar(latN[:, t, 0:DQ], latN[:, t, 0:DQ], rstat[:, t:t + 1], None, ALU.mult)
                V.tensor_scalar(latN[:, t, DQ:DQ + DKV], latN[:, t, DQ:DQ + DKV], rstat[:, 4 + t:5 + t], None,
                                ALU.mult).then_inc(lat_scaled, 1)
            low(slab_at["iq", 0] + 2)
            ready(("iq", 1))
            V.tensor_copy(iqT[:, 2:4, :], bank(("iq", 1))[:, :, :]).then_inc(taken["V"], 1)
            low(slab_at["iq", 1] + 2)
            ready("ik")
            V.tensor_copy(ikT[:, :], bank("ik")[:, 0, :])
            V.tensor_copy(iw, bank("ik")[:, 1, 0:32].rearrange("p (t h) -> p t h", h=8)).then_inc(taken["V"], 1)
            low(slab_at["ik",] + 2)
            for i in range(3):
                dve.wait_ge(lat_high, i + 1)
                for b in range(2 if i < 2 else 1):
                    c = 2 * i + b
                    ins = rest(latL[:, c, :], bank(("latT", i))[:, b, :], latH[:, c, :], gains[:, 56 + c:57 + c])
                ins.then_inc(taken["V"], 1)
            dve.wait_ge(s_strip0, 16)
            n = 0

            def iscore_of(i):
                return iscore[:, TRI[i] - P:TRI[i] - P + (i + 1) * P]

            for i in range(1, NT):
                for h in range(8):
                    dve.wait_ge(index_taken, n + 1)
                    r = relu[:, n % 2, 0:(i + 1) * P]
                    if h == 0:
                        ins = V.tensor_scalar(iscore_of(i), r, iw[:, i, h:h + 1], None, ALU.mult)
                    else:
                        dve.wait_ge(index_added, n)
                        ins = V.scalar_tensor_tensor(iscore_of(i), r, iw[:, i, h:h + 1], iscore_of(i), ALU.mult, ALU.add)
                    ins.then_inc(index_added, 1)
                    n += 1
                dve.wait_ge(index_added, n)
                d = iscore[:, TRI[i] - P + i * P:TRI[i] - P + (i + 1) * P]
                link(V.tensor_tensor(d, d, strip0[:, T - P:], ALU.add))

            rounds = [(i, k) for i in range(1, NT) for k in range(TOPK // 8)]

            def select(first, count):
                for i, k in rounds[first:first + count]:
                    w = iscore_of(i)
                    link(V.max(top8, w))
                    link(V.match_replace(w, top8, w, FILL))
                    if k == TOPK // 8 - 1:
                        ins = V.tensor_scalar(selb[:, TRI[i] - P:TRI[i] - P + (i + 1) * P], w, FILL, NEG,
                                              ALU.not_equal, ALU.mult)
                        ins.then_inc(selection_ready, 1)

            def softmax_in(n, slot, bias_of, scale=1.0):
                for i in range(NT):
                    cols = (i + 1) * P
                    dve.wait_ge(score_ready, n + i + 1)
                    V.tensor_tensor_reduce(out=probs[:, slot, TRI[i]:TRI[i] + cols], in0=S[(n + i) % 2][:, 0:cols],
                                           in1=bias_of(i, cols), scale=scale, scalar=-3.0e38, op0=ALU.add, op1=ALU.max,
                                           accum_out=rowmax[:, 4 * slot + i:4 * slot + i + 1]).then_inc(score_taken, 1)
                dve.wait_ge(score_taken, n + NT)
                V.tensor_scalar(negmax[:, 4 * slot:4 * slot + 4], rowmax[:, 4 * slot:4 * slot + 4], -1.0, None,
                                ALU.mult).then_inc(negmax_ready, 1)

            def normalise(u, slot, gate=None):
                dve.wait_ge(exp_done, u + 1)
                r = rtotal[:, 4 * slot:4 * slot + 4]
                ins = V.reciprocal(r, total[:, 4 * slot:4 * slot + 4])
                if gate is not None:
                    link(ins)
                    ins = V.tensor_tensor(r, r, gate, ALU.mult)
                link(ins)
                for i in range(NT):
                    t = probs[:, slot, TRI[i]:TRI[i] + (i + 1) * P]
                    ins = V.tensor_scalar(t, t, rtotal[:, 4 * slot + i:4 * slot + i + 1], None, ALU.mult)
                ins.then_inc(probs_ready, 1)

            def head_low(att):
                dve.wait_ge(attended_high, att + 1)
                V.tensor_tensor(oTL[:, att % 8, :], OT[:, :], oTH[:, att % 8, :].bitcast(F32), ALU.subtract).then_inc(attended_taken, 1)

            for p in range(4):
                s = slab_at["uq", p]
                rotate(("m2", p), qrT)
                low(s + 2)
                if p:
                    for h in range(2):
                        head_low(2 * (p - 1) + h)
                if not p:
                    low(s + 3)
                for h in range(2):
                    softmax_in((2 * p + h) * NT, h, lambda i, cols: strip0[:, T - cols:], MLA_SCALE)
                if p:
                    low(s + 3)
                for h in range(2):
                    normalise(2 * p + h, h)
                select(4 * p, 4)

            def merge(b):
                for n in range(GROUPS):
                    low(slab_at["bg", b, n] + 2)
                    if n == 0:
                        for h in range(2):
                            head_low(8 * b + 6 + h)
                    if b == 0:
                        select(16 + 8 * n, 4)
                    if b == 2 and n:
                        merged_low(n - 1)
                    ready(("bp", b, n))
                    dve.wait_ge(taken["A"], taken_count[product_at["bg", b, n]])
                    if b:
                        k = (b - 1) * GROUPS + n
                        if k:
                            dve.wait_ge(merge_added, k)
                        ins = V.tensor_tensor(gated[:, :, :], bank(("bp", b, n))[:, :, :], sig[:, :, :], ALU.mult)
                    else:
                        ins = V.tensor_tensor(merged[:, 2 * n:2 * n + 2, :], bank(("bp", b, n))[:, :, :], sig[:, :, :], ALU.mult)
                    ins.then_inc(taken["V"], 1)
                    low(slab_at["bp", b, n] + 2)
                    if b == 0:
                        select(20 + 8 * n, 4)
                if b == 2:
                    merged_low(GROUPS - 1)

            def merged_low(n):
                dve.wait_ge(merged_high, n + 1)
                c = slice(2 * n, 2 * n + 2)
                V.tensor_tensor(mgL[:, c, :], merged[:, c, :], mgH[:, c, :].bitcast(F32), ALU.subtract).then_inc(merged_ready, 1)

            merge(0)
            for p in range(4):
                low(slab_at["dq", p] + 2)
                ready(("dk", p))
                V.tensor_copy(kT[:, :, :], bank(("dk", p))[:, :, :]).then_inc(taken["V"], 1)
                low(slab_at["dk", p] + 2)
                if p:
                    for h in range(2):
                        head_low(8 + 2 * (p - 1) + h)
                if not p:
                    low(slab_at["dv", p] + 2)
                for h in range(2):
                    u = 8 + 2 * p + h
                    dve.wait_ge(strips_loaded[p % 2], 16 * (p // 2 + 1))
                    dve.wait_ge(biased_ready, 2 * p + h + 1)

                    def bias(i, cols, h=h):
                        return biased[:, h, TRI[i]:TRI[i] + cols] if i else strips[:, p % 2, h, T - cols:]
                    softmax_in(u * NT, h, bias)
                for h in range(2):
                    normalise(8 + 2 * p + h, h)
                if p:
                    low(slab_at["dv", p] + 2)
            merge(1)

            for t in flatH + flatL:
                V.memset(t[:, FLAT:].bitcast(F32), 0.0)
            low(slab_at["kc",] + 2)
            for kv, src in enumerate((kcT, vcT)):
                name = ("kc", "vc")[kv]
                dve.wait_ge(taken["A"], taken_count[product_at[name]])
                if kv:
                    dve.wait_ge(flat_split, 1)
                for r in range(2):
                    row = src[:, r, :]
                    window = bass.AP(row.tensor, row.offset, [row.ap[0], (1, 32), (16, NC)])
                    ins = V.tensor_tensor(flat_[:, r, :, :], window, posT[:, kv * 32:(kv + 1) * 32].unsqueeze(2).broadcast_to((P, 32, NC)), ALU.add)
                ins.then_inc(flat_ready, 1)
                dve.wait_ge(flat_high, kv + 1)
                vh, vl = (t[kv][:, 0:FLAT].rearrange("p (l c) -> p l c", c=2 * NC) for t in (flatH, flatL))
                for r in range(2):
                    f = (slice(None), slice(None), slice(r * NC, (r + 1) * NC))
                    ins = V.tensor_tensor(vl[f], flat_[:, r, :, :], vh[f].bitcast(F32), ALU.subtract)
                ins.then_inc(flat_split, 1)
                if kv == 0:
                    low(slab_at["vc",] + 2)
            low(slab_at["ng",] + 2)
            for kv in range(2):
                for c in range(4):
                    low(slab_at["cw", kv, c] + 2)
            dve.wait_ge(cmp2_loaded, 32)
            for p in range(4):
                r = p // 2
                low(slab_at["nq", p] + 2)
                if p == 0:
                    ready("hidT")
                    V.tensor_copy(hid[:, :, :, :].rearrange("p v k c -> p (v k c)"), bank("hidT")[:, 0, 0:8 * NC]).then_inc(taken["V"], 1)
                if p % 2 == 0:
                    ready(("kk", r))
                    V.tensor_copy(kT[:, :, :], bank(("kk", r))[:, :, :]).then_inc(taken["V"], 1)
                    low(slab_at["kk", r] + 2)
                if p == 0:
                    ready("cmp")
                    V.tensor_copy(kcmpT[:, :], bank("cmp")[:, 0, 0:2 * NC])
                    V.tensor_copy(vcmp[0:NC, :, :], bank("cmp")[0:NC, 1, 0:2 * P].rearrange("p (r c) -> p r c", c=P)).then_inc(taken["V"], 1)
                if p:
                    for h in range(2):
                        head_low(16 + 2 * (p - 1) + h)
                if p % 2 == 0:
                    low(slab_at["vv", r] + 2)
                n = TILE_NSA + NSA_TILES * p
                dve.wait_ge(strips_loaded[p % 2], 16 * (p // 2 + 3))
                for h in range(2):
                    for w in range(2):
                        softmax_in(n, 2 * h + w, lambda i, cols: strips[:, p % 2, h, T - cols:])
                        n += NT
                for h in range(2):
                    dve.wait_ge(score_ready, n + 1)
                    t = probC[:, h, :, 0:NC]
                    m = maxC[:, 4 * h:4 * h + 4]
                    V.tensor_tensor(t, S[n % 2][:, 0:P].rearrange("p (t c) -> p t c", c=32)[:, :, 0:NC], late[:, :, :], ALU.add).then_inc(score_taken, 1)
                    n += 1
                    dve.wait_ge(score_taken, n)
                    link(V.tensor_reduce(m, t, AX, ALU.max))
                    link(V.tensor_scalar(m, m, -1e20, None, ALU.max))
                    V.tensor_tensor(t, t, m.unsqueeze(2).broadcast_to((P, NT, NC)), ALU.subtract).then_inc(cmpmax_ready, 1)
                for h in range(2):
                    for w in range(2):
                        u = 2 * h + w
                        c = (1 + w) * 8 + 2 * p + h
                        normalise(16 + 4 * p + u, u, gateN[:, :, c])
                for h in range(2):
                    dve.wait_ge(cmpexp_done, 2 * p + h + 1)
                    m, s_, q = (x[:, 4 * h:4 * h + 4] for x in (maxC, totC, rC))
                    link(V.tensor_reduce(s_, probC[:, h, :, 0:NC], AX, ALU.add))
                    link(V.tensor_scalar(m, s_, 0.0, None, ALU.is_equal))
                    link(V.tensor_tensor(s_, s_, m, ALU.add))
                    link(V.reciprocal(q, s_))
                    link(V.tensor_tensor(q, q, gateN[:, :, 2 * p + h], ALU.mult))
                    t = probC[:, h, :, 0:NC]
                    V.tensor_tensor(t, t, q.unsqueeze(2).broadcast_to((P, NT, NC)), ALU.mult).then_inc(probs_ready, 1)
            merge(2)

            dve.wait_ge(memsum_ready, 2)
            root_arg(nstat[:, 0:2], stat[:, 0:2], D).then_inc(memroot_ready, 1)
            dve.wait_ge(root_done, 6)
            link(V.reciprocal(rstat[:, 0:2], nstat[:, 0:2]))
            for t in range(2):
                V.tensor_scalar(memN[:, t, :], memN[:, t, :], rstat[:, t:t + 1], None, ALU.mult).then_inc(mem_scaled, 1)

            def post(j, gain, roots):
                dve.wait_ge(post_sum[j], 1)
                root_arg(rstd[:, :], PT[:, :], D).then_inc(post_arg[j], 1)
                dve.wait_ge(root_done, roots)
                link(V.reciprocal(rstd[:, :], rstd[:, :]))
                for c in range(KD):
                    V.scalar_tensor_tensor(yT[:, c, :], yT[:, c, :], gains[:, gain * KD + c:gain * KD + c + 1], rstd[:, :],
                                           ALU.mult, ALU.mult).then_inc(post_scaled[j], 1)
                    if c % 2 and j:
                        dve.wait_ge(post_scaled[j], c + 1)
                        V.tensor_tensor(XT[:, c, :], XT[:, c, :], yT[:, c, :], ALU.add).then_inc(resid_dve[j], 1)

            def pre(j, gain, roots):
                dve.wait_ge(presum[j], KD)
                root_arg(rstd[:, :], OT[:, :], D).then_inc(pre_arg[j], 1)
                dve.wait_ge(root_done, roots)
                link(V.reciprocal(rstd[:, :], rstd[:, :]))

                for c in range(KD):
                    if c >= 2:
                        dve.wait_ge(nhid_ready[j], c - 1)
                    V.scalar_tensor_tensor(normed[:, c % 2, :], XT[:, c, :], gains[:, gain * KD + c:gain * KD + c + 1], rstd[:, :],
                                           ALU.mult, ALU.mult).then_inc(normed_ready[j], 1)

            for n in range(2):
                low(slab_at["wo", n] + 2)
            for i in range(2):
                dve.wait_ge(mem_high, i + 1)
                for c in range(4):
                    k = 4 * i + c
                    ins = rest(memL[:, k, :], bank(("mem", i))[:, c // 2, c % 2 * MEM:(c % 2 + 1) * MEM], memH[:, k, :], gains[:, 24 + k:25 + k])
                ins.then_inc(taken["V"], 1)
            for n in range(2, GROUPS):
                low(slab_at["wo", n] + 2)
            post(0, 1, 7)
            for n in range(GROUPS):
                ready(("ck", n))
                V.tensor_copy(kxT[:, 2 * n:2 * n + 2, :], bank(("ck", n))[:, :, 0:MEM]).then_inc(taken["V"], 1)
                low(slab_at["ck", n] + 2)
                if n == 1:
                    pre(0, 2, 8)
            for n in range(GROUPS):
                low(slab_at["cv", n] + 2)

            def cross_low(n):
                for b in range(2):
                    c = 2 * n + b
                    dve.wait_ge(catt_high, c + 1)
                    V.tensor_tensor(coL[:, c, :], (OT, S[1])[b][:, :], coH[:, c, :].bitcast(F32), ALU.subtract).then_inc(catt_taken, 1)

            for n in range(GROUPS):
                low(slab_at["cq", n] + 2)
                if n:
                    cross_low(n - 1)
                for i in range(NT):
                    m = n * NT + i
                    dve.wait_ge(cross_ready, m + 1)
                    V.tensor_reduce(negmax[:, i:i + 1], S[m % 2][:, 0:MEM], AX, ALU.max, negate=True).then_inc(cmax_ready, 1)
                dve.wait_ge(cross_taken, NT * (n + 1))
                V.reciprocal(rtotal[:, 0:4], total[:, 0:4]).then_inc(crt_ready, 1)
            cross_low(3)
            for n in range(GROUPS):
                low(slab_at["co", n] + 2)
            post(1, 4, 9)
            pre(1, 5, 10)

            def up_low(n):
                dve.wait_ge(up_high, n + 1)
                c = slice(2 * (n % 8), 2 * (n % 8) + 2)
                V.tensor_tensor(h1L[:, c, :], h1[:, n % 2, :, :], h1H[:, c, :].bitcast(F32), ALU.subtract).then_inc(up_ready, 1)

            for f in range(2):
                for n in range(8):
                    low(slab_at["up", f, n] + 2)
                    if n:
                        up_low(8 * f + n - 1)
                up_low(8 * f + 7)
                for n in range(GROUPS):
                    s = slab_at["down", f, n, 0]
                    low(s + 2)
                    if f:
                        ready(("down", f, n))
                        y = yT[:, 2 * n:2 * n + 2, :]
                        V.tensor_tensor(y, bank(("down", f, n))[:, :, :], y, ALU.add).then_inc(taken["V"], 1)
                    low(s + 3)
            post(2, 6, 11)

        @block.gpsimd
        def _(pool):
            Q = nc.gpsimd
            Q.memset(ones[:, :], 1.0).then_inc(pool_step, 1)
            pool.wait_ge(taken["V"], 1)
            pool.dma_start(scratch, biasRow[:, :].unsqueeze(1).broadcast_to((16, P, T + P))).then_inc(scratch_written, 16)

            def load_strips(k):
                src = bass.AP(scratch.tensor, 2 * k * P * (T + P) + P - 1, [(T + P - 1, P), (P * (T + P), 2), (1, T)])
                pool.dma_start(strips[:, k % 2, :, :], src).then_inc(strips_loaded[k % 2], 16)

            pool.wait_ge(scratch_written, 16)
            pool.wait_ge(product_ready, ready_at["m4", 3])
            load_strips(0)
            load_strips(1)
            pool.wait_ge(selection_ready, NT - 1)
            for p in range(4):
                if p:
                    pool.wait_ge(score_taken, (UNITS_MLA + 2 * p) * NT)
                    if p < 3:
                        load_strips(p + 1)
                pool.wait_ge(strips_loaded[p % 2], 16 * (p // 2 + 1))
                for h in range(2):
                    for i in range(1, NT):
                        cols = (i + 1) * P
                        ins = Q.tensor_tensor(biased[:, h, TRI[i]:TRI[i] + cols], strips[:, p % 2, h, T - cols:],
                                              selb[:, TRI[i] - P:TRI[i] - P + cols], ALU.add)
                    ins.then_inc(biased_ready, 1)

            def merge(b):
                for n in range(GROUPS):
                    pool.wait_ge(taken["V"], taken_count[product_at["bp", b, n]])
                    m = merged[:, 2 * n:2 * n + 2, :]
                    Q.tensor_tensor(m, m, gated[:, :, :], ALU.add).then_inc(merge_added, 1)

            merge(1)
            pool.wait_ge(product_ready, ready_at["hid", 1])
            load_strips(4)
            load_strips(5)
            for p in range(4):
                if p < 2:
                    pool.wait_ge(score_taken, TILE_NSA + NSA_TILES * (p + 1))
                    load_strips(6 + p)
            merge(2)

            def hidden_low(j):
                for c in range(KD):
                    pool.wait_ge(nhigh_ready[j], c + 1)
                    Q.tensor_tensor(hTL[:, c, :], normed[:, c % 2, :], hTH[:, c, :].bitcast(F32), ALU.subtract).then_inc(nhid_ready[j], 1)

            def residual(j):
                for c in range(0, KD, 2 if j else 1):
                    pool.wait_ge(post_scaled[j], c + 1)
                    Q.tensor_tensor(XT[:, c, :], XT[:, c, :], yT[:, c, :], ALU.add).then_inc(resid_ready[j], 1)

            pool.wait_ge(taken["A"], taken_count[product_at["xt", 3]])
            residual(0)
            hidden_low(0)
            for n in range(GROUPS):
                pool.wait_ge(crt_ready, n + 1)
                for i in range(NT):
                    ins = Q.tensor_scalar(probX[:, i, :], probX[:, i, :], rtotal[:, i:i + 1], None, ALU.mult)
                ins.then_inc(cprobs_ready, 1)
            residual(1)
            hidden_low(1)
            for n in range(16):
                pool.wait_ge(taken["A"], taken_count[product_at["up", n // 8, n % 8]])
                t = h1[:, n % 2, :, :]
                Q.tensor_tensor(t, t, t, ALU.mult).then_inc(up_squared, 1)
            residual(2)


INS = ("x", "mem", "positions", "rel_bias", "norm_gains", "w_in", "mla_q_norm", "mla_kv_norm", "mla_w_uq",
       "mla_w_ukv", "nsa_cmp_pos", "nsa_cmp_w1", "nsa_cmp_w2", "w_branch", "w_out", "cross_wq", "cross_wkv",
       "cross_wo", "mlp_w1", "mlp_w2")


def kernel(**inputs):
    import concourse.bacc as bacc
    from concourse.bass_utils import run_bass_kernel_spmd

    nc = bacc.Bacc("TRN2", target_bir_lowering=False, num_devices=1)
    given = {name: np.ascontiguousarray(inputs[name]) for name in INS}
    given.update(shape_constants())
    aps = {name: nc.dram_tensor(f"in_{name}", v.shape, mybir.dt.from_np(v.dtype), kind="ExternalInput").ap()
           for name, v in given.items()}
    out = nc.dram_tensor("out", (1, T, D), F32, kind="ExternalOutput").ap()
    layer(nc, aps, out)
    r = run_bass_kernel_spmd(nc, [{f"in_{name}": v for name, v in given.items()}], core_ids=[0])
    return r.results[0]["out"]
```

```python
from contextlib import ExitStack

import numpy as np
import concourse.bass as bass
import concourse.mybir as mybir

F32 = mybir.dt.float32
F32R = mybir.dt.float32r
I32 = mybir.dt.int32
ALU = mybir.AluOpType
ACT = mybir.ActivationFunctionType
AX = mybir.AxisListType.X

P = 128
T = 512
NT = T // P
D = 1024
KD = D // P
EPS = 1e-6
NEG = -1e30
FILL = -3e38
TOPK = 128
DQ, DKV, ROPE = 384, 256, 64
MLA_SCALE = (128 + ROPE) ** -0.5
HEAD_SCALE = 128 ** -0.5
CROSS_SCALE = 256 ** -0.5
MEM = 256
NC = T // 16 - 1
FF = 4 * D
SW = 256
GROUPS = D // SW
WIDTHS = (DQ, DKV, ROPE, D, D, D, 512, 64, 8, D, 256, 256, 256, 256, 256, 256, 24, 3 * D)
COLS = [sum(WIDTHS[:i]) for i in range(len(WIDTHS))]
(C_LAT, _, _, C_DQ, C_DK, C_DV, C_IQ, C_IK, _, C_NQ, C_KC, C_VC, C_KS, C_VS, C_KW, C_VW, C_NG,
 C_BG) = COLS
TRI = [P * sum(range(1, i + 1)) for i in range(NT)]
UNIT = P * NT * (NT + 1) // 2


def shape_constants():
    n = np.arange(T - 1, -1, -1)
    exact = 16
    far = exact + (np.log(np.maximum(n, 1) / exact) / np.log(128 / exact) * exact).astype(np.int64)
    bucket = np.where(n < exact, n, np.minimum(far, 31))
    onehot = (bucket[None, :] == np.arange(32)[:, None]).astype(np.float32)
    row = np.arange(P)
    freq = np.float32(10000.0) ** (-(np.arange(0, ROPE, 2, dtype=np.float32)) / np.float32(ROPE))
    turn = np.stack([freq[row % 32], np.where(row % 64 < 32, -1.0, 1.0)], 1).astype(np.float32)
    strip = np.zeros((P, T), np.float32)
    strip[:, T - P:] = np.where(row[None, :] > row[:, None], NEG, 0.0)
    t = np.arange(T).reshape(NT, P).T
    late = (np.arange(NC) * 16 + 31)[None, None, :] > t[:, :, None]
    return {
        "c_ident": np.eye(P, dtype=np.float32),
        "c_onehot": onehot,
        "c_turn": turn,
        "c_strip": strip,
        "c_late": np.where(late, np.float32(NEG), np.float32(0.0)).astype(np.float32),
    }


def layer(nc, a, out):
    ctx = ExitStack()
    KB = 1024
    base = -(-nc.sbuf_base // 32) * 32

    def at(name, shape, kb, dt=F32):
        return nc.alloc_sbuf_tensor_at(name, shape, dt, offset=base + int(kb * KB))

    def sem(name):
        return ctx.enter_context(nc.semaphore(name))

    with ctx:
        raw = [at(f"raw{i}", [P, KD, SW], 8 * i) for i in range(2)]
        wh = [at(f"weight_high{i}", [P, KD, SW], 16 + 8 * i, F32R) for i in range(2)]
        wl = [at(f"weight_low{i}", [P, KD, SW], 32 + 8 * i, F32R) for i in range(2)]
        hTH = at("hidden_high", [P, KD, T], 48, F32R)
        hTL = at("hidden_low", [P, KD, T], 64, F32R)
        oTH = at("branch_out_high", [P, KD, T], 80, F32R)
        oTL = at("branch_out_low", [P, KD, T], 96, F32R)
        merged = at("merged", [P, KD, T], 112)
        qT = at("qT", [P, 2, T], 128)
        kT = at("kT", [P, 2, T], 132)
        vN = at("vN", [P, NT, 2 * P], 136)
        probs = at("probs", [P, 4, UNIT], 140)
        probsT = at("probsT", [P, 3, T], 160)
        xN = at("x_rows", [P, NT, D], 96)
        latN = at("latent_rows", [P, NT, 704], 80)
        latH = at("latent_high", [P, 5, T], 170, F32R)
        latL = at("latent_low", [P, 5, T], 180, F32R)
        qrT = at("q_rope", [P, T], 190)
        krT = at("k_rope", [P, T], 192)
        cosT = at("cosT", [P, T], 194)
        sinT = at("sinT", [P, T], 196)
        ropeTmp = at("rope_tmp", [P, T], 198)
        strip0 = at("causal_strip", [P, T], 150)
        posI = at("positions_int", [P, T], 154, I32)
        angle = at("angle", [P, T], 156)
        turns = at("turns", [P, T], 158)
        iqT = at("index_q", [P, 4, T], 112)
        ikT = at("index_k", [P, T], 120)
        iscore = at("index_score", [P, UNIT - P], 152)
        relu = at("index_relu", [P, 2, T], 200)
        selb = at("selection_bias", [P, UNIT - P], 200)
        strips = at("bias_strips", [P, 2, 2, T], 170)
        biased = at("selection_strips", [P, 2, UNIT], 178)
        kcT = at("kcT", [P, 2, T], 128)
        vcT = at("vcT", [P, 2, T], 132)
        flat_ = at("flat", [P, 2, 32, NC], 136)
        FLAT = 32 * 2 * NC
        flatH = [at(f"flat_high{kv}", [P, FLAT + P - 2 * NC], 144 + 16.25 * kv, F32R) for kv in range(2)]
        flatL = [at(f"flat_low{kv}", [P, FLAT + P - 2 * NC], 152.125 + 16.25 * kv, F32R) for kv in range(2)]
        hidR = at("cmp_hidden_rows", [2 * NC, 2, SW], 194)
        hid = at("cmp_hidden", [P, 2, 2, 2 * NC], 188)
        cmpW2 = at("cmp_w2", [P, 2, 2, P], 189)
        kcmpT = at("k_cmpT", [P, 2 * NC], 191)
        vcmp = at("v_cmp", [32, 2, P], 191.25)
        late = at("cmp_mask", [P, NT, NC], 192.25)
        probC = at("cmp_probs", [P, 2, NT, 32], 192.75)
        gateN = at("nsa_gates", [P, NT, 24], 205.5)
        sig = at("branch_gate", [P, 2, T], 128)
        gated = at("gated", [P, 2, T], 132)
        mgH = at("merged_high", [P, KD, T], 140, F32R)
        mgL = at("merged_low", [P, KD, T], 156, F32R)
        yT = at("y", [P, KD, T], 172)
        square = at("square", [P, 2, 2, T], 188)
        outSquare = [at("out_square", [P, 2, 2, T], 48), square, square]
        rstd = at("rstd", [P, T], 196)
        squareSum = at("square_sum", [P, T], 198)
        XT = at("residual", [P, KD, T], 80)
        xN2 = at("x_rows_again", [P, NT, D], 186)
        memN = at("mem_rows", [P, 2, D], 64)
        memH = at("mem_high", [P, KD, MEM], 96, F32R)
        memL = at("mem_low", [P, KD, MEM], 104, F32R)
        normed = at("normed", [P, 2, T], 201.5)
        kxT = at("cross_k", [P, KD, MEM], 112)
        vxN = at("cross_v", [P, 2, D], 120)
        probX = at("cross_probs", [P, NT, MEM], 132)
        probXT = at("cross_probsT", [P, 2, T], 136)
        coH = at("cross_out_high", [P, KD, T], 140, F32R)
        coL = at("cross_out_low", [P, KD, T], 156, F32R)
        h1H = at("up_high", [P, 16, T], 96, F32R)
        h1L = at("up_low", [P, 16, T], 128, F32R)
        h1 = at("up", [P, 2, 2, T], 160)
        outN = at("out_rows", [P, NT, D], 128)
        ident = at("ident", [P, P], 206)
        small = at("small", [P, 288], 206.5)
        gains = small[:, 0:61]
        posT = small[:, 61:125]
        stat = small[:, 125:133]
        rstat = small[:, 133:141]
        rowmax = small[:, 141:157]
        negmax = small[:, 157:173]
        total = small[:, 173:189]
        rtotal = small[:, 189:205]
        turn = small[:, 205:207]
        top8 = small[:, 207:215]
        maxC = small[:, 215:223]
        totC = small[:, 223:231]
        rC = small[:, 231:239]
        iw = small[:, 239:271].rearrange("p (t h) -> p t h", h=8)
        nstat = small[:, 271:279]
        eps = small[:, 279:280]
        spare = small[:, 280:281]
        gainRows = at("gain_rows", [64, P], 128)
        posRows = at("pos_rows", [64, P], 128.5)
        tab = at("bias_table", [32, 16], 129)
        onehot = at("onehot", [32, T], 130)
        biasRow = at("bias_row", [16, T + P], 132)
        ones = at("ones", [P, P], 205.5)

        def ps(name, shape):
            return ctx.enter_context(nc.psum_tensor(name, shape, F32))

        G = [ps("dense0", [P, 2, T]), ps("dense1", [P, 2, T])]
        S = [ps("score0", [P, T]), ps("score1", [P, T])]
        PT = ps("turned", [P, T])
        OT = ps("attended", [P, T])
        SCORE = [S[0], S[1], PT]
        TURNED = [PT, S[0]]
        ATT = [S[1], OT]

        def flat(tile):
            return tile[:, :, :].rearrange("p k c -> p (k c)")

        def wide(tile, k, c):
            return flat(tile)[:, 0:k * c].rearrange("p (k c) -> p k c", c=c)

        win = a["w_in"][0].rearrange("(k p) c -> p k c", p=P)

        def square_slab(w, c0, c1, k0=0):
            return [(w[:, k0:k0 + KD, c0:c1], lambda t: t[:, :, 0:c1 - c0])]

        def rows(name, *i):
            w = a[name][0]
            for j in i:
                w = w[j]
            return w.rearrange("(k p) c -> p k c", p=P)

        slabs, slab_at = [], {}

        def slab(name, pieces):
            slab_at[name] = len(slabs)
            slabs.append(pieces)

        slab(("lat", 0), square_slab(win, 0, 256))
        slab(("lat", 1), square_slab(win, 256, 512))
        slab(("lat", 2), [(win[:, :, 512:512 + P], lambda t: t[:, :, 0:P]),
                          (win[:, :, C_IK + 64:C_IK + 72], lambda t: t[:, :, P:P + 8]),
                          (win[:, :, C_NG:C_NG + 24], lambda t: t[:, :, P + 8:P + 32])])
        slab(("kr",), square_slab(win, C_LAT + DQ + DKV, C_LAT + DQ + DKV + ROPE))
        slab(("iq", 0), square_slab(win, C_IQ, C_IQ + 256))
        slab(("iq", 1), square_slab(win, C_IQ + 256, C_IQ + 512))
        slab(("ik",), square_slab(win, C_IK, C_IK + 64))
        for p in range(4):
            slab(("uq", p), [(rows("mla_w_uq")[:, :, p * 384:(p + 1) * 384], lambda t: wide(t, 3, 384))])
            slab(("ukv", p), [(rows("mla_w_ukv")[:, :, p * 512:(p + 1) * 512], lambda t: wide(t, 2, 512))])

        def merge_slabs(b):
            for n in range(GROUPS):
                slab(("bg", b, n), square_slab(win, C_BG + b * D + n * SW, C_BG + b * D + (n + 1) * SW))
                slab(("bp", b, n), square_slab(rows("w_branch", b), n * SW, (n + 1) * SW))

        merge_slabs(0)
        for p in range(4):
            for name, c in (("dq", C_DQ), ("dk", C_DK), ("dv", C_DV)):
                slab((name, p), square_slab(win, c + p * SW, c + (p + 1) * SW))
        merge_slabs(1)
        slab(("kc",), square_slab(win, C_KC, C_KC + SW))
        slab(("vc",), square_slab(win, C_VC, C_VC + SW))

        def nsa_slab(name, i):
            if name == "cw":
                slab(("cw", *i), square_slab(rows("nsa_cmp_w1", i[0]), 0, SW, i[1] * KD))
            elif name == "nq":
                slab(("nq", i), square_slab(win, C_NQ + i * SW, C_NQ + (i + 1) * SW))
            else:
                c0, c1 = {"kk": (C_KS, C_KW), "vv": (C_VS, C_VW)}[name]
                slab((name, i), [
                    (win[:, :, c0 + i * P:c0 + (i + 1) * P], lambda t: t[:, :, 0:P]),
                    (win[:, :, c1 + i * P:c1 + (i + 1) * P], lambda t: t[:, :, P:2 * P])])

        NSA_BEGIN = [("nq", 0), ("cw", (0, 0)), ("kk", 0), ("cw", (0, 1)), ("cw", (0, 2)), ("cw", (0, 3)),
                     ("cw", (1, 0)), ("cw", (1, 1)), ("cw", (1, 2)), ("cw", (1, 3)), ("vv", 0)]
        for name, i in NSA_BEGIN:
            nsa_slab(name, i)
        for name, i in (("nq", 1), ("nq", 2), ("kk", 1), ("vv", 1), ("nq", 3)):
            nsa_slab(name, i)
        merge_slabs(2)
        for n in range(GROUPS):
            slab(("wo", n), square_slab(rows("w_out"), n * SW, (n + 1) * SW))
        for n in range(GROUPS):
            slab(("ck", n), square_slab(rows("cross_wkv"), n * SW, (n + 1) * SW))
        for n in range(GROUPS):
            slab(("cv", n), square_slab(rows("cross_wkv"), D + n * SW, D + (n + 1) * SW))
        for n in range(GROUPS):
            slab(("cq", n), square_slab(rows("cross_wq"), n * SW, (n + 1) * SW))
        for n in range(GROUPS):
            slab(("co", n), square_slab(rows("cross_wo"), n * SW, (n + 1) * SW))
        for f in range(2):
            for n in range(8):
                c = f * 2048 + n * SW
                slab(("up", f, n), square_slab(rows("mlp_w1"), c, c + SW))
            for n in range(GROUPS):
                for k in range(2):
                    slab(("down", f, n, k), square_slab(rows("mlp_w2"), n * SW, (n + 1) * SW, f * 16 + k * KD))
        SLABS = len(slabs)
        landed, counts = [], [0, 0]
        for s, pieces in enumerate(slabs):
            counts[s % 2] += 16 * len(pieces)
            landed.append(counts[s % 2])

        halved = {slab_at[name] for name in slab_at if name[0] in ("cw", "ck", "cv")}
        halved |= {slab_at[name] for name in (("lat", 0), ("kk", 0), ("vv", 0), ("cq", 0), ("wo", 1),
                                              ("co", 2), ("co", 3))}
        split_at = [s + 1 + sum(h <= s for h in halved) for s in range(SLABS)]

        def half_pieces(s, dst, src):
            return [(dst[:, k:k + KD // 2, :], src[:, k:k + KD // 2, :]) for k in (0, KD // 2)]

        def split_pieces(s, dst, src):
            def doubled(c, n, c0, width=128):
                return [(dst[:, :, c + h * 64:c + h * 64 + n], src[:, :, c0:c0 + n]) for h in range(width // 64)]
            if s == slab_at["lat", 2]:
                return [(dst[:, :, 0:P + 32], src[:, :, 0:P + 32])]
            if s == slab_at["kr",]:
                return doubled(0, 64, 0) + doubled(128, 32, 32) + doubled(160, 32, 0)
            if slab_at["uq", 0] <= s < slab_at["uq", 0] + 8 and (s - slab_at["uq", 0]) % 2 == 0:
                d = wide(dst, 3, 512).rearrange("p k (q h c) -> p k q h c", q=2, h=2, c=128)[:, :, 0]
                e = wide(dst, 3, 512)[:, :, 256:512].rearrange("p k (q h c) -> p k q h c", q=2, h=2)
                r = wide(src, 3, 384).rearrange("p k (h c) -> p k h c", c=192)
                return [(d, r[:, :, :, 0:128]), (e[:, :, 0], r[:, :, :, 128:192]),
                        (e[:, :, 1, :, 0:32], r[:, :, :, 160:192]), (e[:, :, 1, :, 32:64], r[:, :, :, 128:160])]
            if slab_at["ukv", 0] <= s < slab_at["ukv", 0] + 8 and (s - slab_at["ukv", 0]) % 2 == 0:
                return [(wide(dst, 2, 512), wide(src, 2, 512))]
            if s == slab_at["ik",]:
                return doubled(0, 64, 0)
            return [(dst[:, :, :], src[:, :, :])]

        product_at, takers, ready_at, used_at = {}, [], {}, {}
        events = [0]

        def part(s):
            events[0] += 1
            used_at[s] = events[0]

        def product(name, taker, s=None):
            product_at[name] = len(takers)
            takers.append(taker)
            part(s)
            ready_at[name] = events[0]

        product("setup", "V")
        for i in range(4):
            product(("x", i), "V")
        for i in range(3):
            product(("lat", i), "A", slab_at["lat", i])
        product("krope", "V", slab_at["kr",])
        product(("iq", 0), "A", slab_at["iq", 0])
        product(("iq", 1), "V", slab_at["iq", 1])
        product("ik", "V", slab_at["ik",])
        for i in range(3):
            product(("latT", i), "V")
        for p in range(4):
            product(("m1", p), "A", slab_at["uq", p])
            product(("m2", p), "V", slab_at["uq", p])
            product(("m3", p), "A", slab_at["ukv", p])
            product(("m4", p), "A", slab_at["ukv", p])

        def merge_products(b):
            for n in range(GROUPS):
                product(("bg", b, n), "A", slab_at["bg", b, n])
                product(("bp", b, n), "V", slab_at["bp", b, n])

        merge_products(0)
        for p in range(4):
            product(("dq", p), "A", slab_at["dq", p])
            product(("dk", p), "V", slab_at["dk", p])
            product(("dv", p), "A", slab_at["dv", p])
        merge_products(1)
        product("kc", "A", slab_at["kc",])
        product("vc", "A", slab_at["vc",])
        for name, i in NSA_BEGIN:
            if name == "cw":
                part(slab_at["cw", *i])
                ready_at["hid", i[0]] = events[0]
            else:
                product((name, i), {"nq": "A", "kk": "V", "vv": "A"}[name], slab_at[name, i])
        product("hidT", "V")
        product("cmp", "V")
        for name, i in (("nq", 1), ("nq", 2), ("kk", 1), ("vv", 1), ("nq", 3)):
            product((name, i), {"nq": "A", "kk": "V", "vv": "A"}[name], slab_at[name, i])
        merge_products(2)
        for n in range(GROUPS):
            if n < 2:
                product(("xt", 2 * n), "A")
                product(("xt", 2 * n + 1), "V")
            product(("wo", n), "A", slab_at["wo", n])
        for n in range(GROUPS):
            product(("ck", n), "V", slab_at["ck", n])
        for n in range(GROUPS):
            product(("cv", n), "A", slab_at["cv", n])
        for n in range(GROUPS):
            product(("cq", n), "A", slab_at["cq", n])
        for n in range(GROUPS):
            product(("co", n), "A", slab_at["co", n])
        for f in range(2):
            for n in range(8):
                product(("up", f, n), "A", slab_at["up", f, n])
            for n in range(GROUPS):
                part(slab_at["down", f, n, 0])
                product(("down", f, n), "A" if f == 0 else "V", slab_at["down", f, n, 1])
        for i in range(4):
            product(("out", i), "A")
        taken_count = [takers[:i + 1].count(t) for i, t in enumerate(takers)]

        UNITS_MLA, UNITS_DSA = 8, 16
        NSA_TILES = 4 * NT + 2
        TILE_NSA = UNITS_DSA * NT
        INDEX_TILES = 3 * 8

        s_setup = sem("setup_loaded")
        s_x = [sem(f"x_loaded{t}") for t in range(NT)]
        s_pos = sem("positions_loaded")
        s_strip0 = sem("causal_strip_loaded")
        loaded = [sem("slab_loaded0"), sem("slab_loaded1")]
        high_ready = sem("slab_high_ready")
        low_ready = sem("slab_low_ready")
        product_ready = sem("product_ready")
        taken = {"A": sem("product_taken_by_act"), "V": sem("product_taken_by_dve")}
        act_step = sem("act_step")
        dve_step = sem("dve_step")
        ones_ready = sem("ones_ready")
        pool_step = sem("pool_step")
        x_scaled = sem("x_rows_scaled")
        xsum_ready = sem("x_square_sums")
        xroot_ready = sem("x_root_arg")
        root_done = sem("root_done")
        hidden_high = sem("hidden_high_ready")
        bias_row_ready = sem("bias_row_ready")
        scratch_written = sem("scratch_written")
        angle_ready = sem("angle_ready")
        sine_ready = sem("sine_ready")
        latsum_ready = sem("latent_square_sums")
        lat_scaled = sem("latent_scaled")
        lat_high = sem("latent_high_ready")
        index_ready = sem("index_scores_ready")
        index_taken = sem("index_scores_taken")
        index_added = sem("index_scores_added")
        selection_ready = sem("selection_ready")
        score_ready = sem("scores_ready")
        score_taken = sem("scores_taken")
        negmax_ready = sem("negmax_ready")
        exp_done = sem("exp_done")
        probs_ready = sem("probs_ready")
        turned_ready = sem("turned_ready")
        probsT_ready = sem("probsT_ready")
        attended_ready = sem("attended_ready")
        attended_high = sem("attended_high")
        attended_taken = sem("attended_taken")
        merge_added = sem("merge_added")
        strips_loaded = [sem("strips_loaded0"), sem("strips_loaded1")]
        biased_ready = sem("biased_ready")
        hid_taken = sem("hidden_rows_taken")
        gates_ready = sem("nsa_gates_ready")
        flat_ready = sem("flat_ready")
        flat_high = sem("flat_high_ready")
        flat_split = sem("flat_split")
        cmp2_loaded = sem("cmp_w2_loaded")
        cmpmax_ready = sem("cmp_max_ready")
        cmpexp_done = sem("cmp_exp_done")
        merged_high = sem("merged_high_ready")
        merged_ready = sem("merged_ready")
        x2_loaded = sem("x_loaded_again")
        mem_loaded = sem("mem_loaded")
        memsum_ready = sem("mem_square_sums")
        memroot_ready = sem("mem_root_arg")
        mem_scaled = sem("mem_scaled")
        mem_turned = sem("mem_turned")
        mem_taken = sem("mem_taken")
        mem_high = sem("mem_high_ready")
        post_sum = [sem(f"post_sum{j}") for j in range(3)]
        post_scaled = [sem(f"post_scaled{j}") for j in range(3)]
        squared = sem("projection_squares")
        squares_added = sem("squares_added")
        rms_ready = sem("rms_ready")
        resid_ready = [sem(f"residual_ready{j}") for j in range(3)]
        resid_dve = [sem(f"residual_ready_dve{j}") for j in range(3)]
        presq_ready = [sem(f"pre_squares{j}") for j in range(2)]
        presum = [sem(f"pre_sum{j}") for j in range(2)]
        normed_ready = [sem(f"normed_ready{j}") for j in range(2)]
        nhigh_ready = [sem(f"normed_high{j}") for j in range(2)]
        nhid_ready = [sem(f"normed_split{j}") for j in range(2)]
        cross_ready = sem("cross_scores_ready")
        cross_taken = sem("cross_scores_taken")
        cmax_ready = sem("cross_max_ready")
        crt_ready = sem("cross_rtotal_ready")
        cprobs_ready = sem("cross_probs_ready")
        cturned_ready = sem("cross_turned_ready")
        cprobsT_ready = sem("cross_probsT_ready")
        catt_ready = sem("cross_attended_ready")
        catt_high = sem("cross_attended_high")
        catt_taken = sem("cross_attended_taken")
        up_relu = sem("up_relu")
        up_squared = sem("up_squared")
        up_high = sem("up_high_ready")
        up_ready = sem("up_ready")
        downsq_ready = sem("down_squares")
        out_written = sem("out_written")

        scratch = nc.dram_tensor("bias_scratch", (16, P, T + P), F32, kind="Internal").ap()
        block = ctx.enter_context(nc.Block())

        def out_row(w):
            return w[0].rearrange("(t p) d -> p t d", p=P)

        @block.sync
        def _(sp):
            for t in range(NT):
                sp.dma_start(xN[:, t, :], out_row(a["x"])[:, t, :]).then_inc(s_x[t], 16)
            sp.dma_start(ident[:, :], a["c_ident"]).then_inc(s_setup, 16)
            sp.dma_start(gainRows[0:56, :], a["norm_gains"][0].rearrange("n (k p) -> (n k) p", p=P)).then_inc(s_setup, 16)
            sp.dma_start(gainRows[56:59, :], a["mla_q_norm"][0].rearrange("(k p) -> k p", p=P)).then_inc(s_setup, 16)
            sp.dma_start(gainRows[59:61, :], a["mla_kv_norm"][0].rearrange("(k p) -> k p", p=P)).then_inc(s_setup, 16)
            sp.dma_start(posRows[:, :], a["nsa_cmp_pos"][0].rearrange("n l d -> (n l) d")).then_inc(s_setup, 16)
            sp.dma_start(tab[:, :], a["rel_bias"]).then_inc(s_setup, 16)
            sp.dma_start(onehot[:, :], a["c_onehot"]).then_inc(s_setup, 16)

            def load(s):
                if s >= 2:
                    sp.wait_ge(low_ready, split_at[s - 2])
                for src, view in slabs[s]:
                    sp.dma_start(view(raw[s % 2]), src).then_inc(loaded[s % 2], 16)

            for s in range(2):
                load(s)
            sp.dma_start(turn, a["c_turn"]).then_inc(s_pos, 16)
            sp.dma_start(posI[:, :], a["positions"][0].partition_broadcast(P)).then_inc(s_pos, 16)
            sp.dma_start(strip0[:, :], a["c_strip"]).then_inc(s_strip0, 16)
            for s in range(2, slab_at["cw", 0, 0]):
                load(s)
            sp.wait_ge(attended_taken, 16)
            sp.dma_start(cmpW2[:, :, :, :].rearrange("p n k d -> p (n k) d"),
                         a["nsa_cmp_w2"][0].rearrange("n (k p) d -> p (n k) d", p=P)).then_inc(cmp2_loaded, 16)
            sp.dma_start(late[:, :, :], a["c_late"]).then_inc(cmp2_loaded, 16)
            for s in range(slab_at["cw", 0, 0], SLABS):
                load(s)
            for i in range(NT):
                sp.wait_ge(taken["A"], taken_count[product_at["out", i]])
                sp.dma_start(out_row(out)[:, :, i * SW:(i + 1) * SW], outN[:, :, i * SW:(i + 1) * SW]).then_inc(out_written, 16)
            sp.wait_ge(out_written, 16 * NT)

        @block.tensor
        def _(pe):
            def free(g):
                if g >= 2:
                    pe.wait_ge(taken[takers[g - 2]], taken_count[g - 2])

            def slab_half(s, half):
                pe.wait_ge(low_ready, split_at[s] - (s in halved and half == 0))

            def blocks3(out_ap, wide_pair, move_pair, first, last):
                (ah, al), (bh, bl) = wide_pair, move_pair
                pe.matmul(out_ap, ah, bh, start=first, stop=False)
                pe.matmul(out_ap, ah, bl, start=False, stop=False)
                return pe.matmul(out_ap, al, bh, start=False, stop=last)

            def t_mode(s, dst, cols, chunks, act, wait_chunk=None, k0=0, k_all=None, w0=0):
                high, low = wh[s % 2], wl[s % 2]
                k_all = k_all or chunks
                slab_half(s, 0)
                for k in range(chunks):
                    if s in halved and k == KD // 2:
                        slab_half(s, 1)
                    if wait_chunk:
                        wait_chunk(k)
                    for b, c in enumerate(cols):
                        mm = blocks3(dst[b], (c(high, w0 + k), c(low, w0 + k)), (act[0][:, k0 + k, :], act[1][:, k0 + k, :]),
                                     k0 + k == 0, k0 + k == k_all - 1)
                return mm

            def n_mode(s, dst, cols, chunks, act, tiles=NT, k0=0):
                high, low = wh[s % 2], wl[s % 2]
                slab_half(s, 0)
                for t in range(tiles):
                    for k in range(chunks):
                        if s in halved and t == 0 and k == KD // 2:
                            slab_half(s, 1)
                        mm = blocks3(dst(t), (act[0][:, k0 + k, t * P:(t + 1) * P], act[1][:, k0 + k, t * P:(t + 1) * P]),
                                     (cols(high, k), cols(low, k)), k == 0, k == chunks - 1)
                return mm

            def two(g):
                return [G[g % 2][:, 0, :], G[g % 2][:, 1, :]]

            def pair_cols(c0=0, c1=P):
                return [lambda t, k: t[:, k, c0:c0 + P], lambda t, k: t[:, k, c1:c1 + P]]

            def tokens_out(g):
                v = G[g % 2][:, :, :].rearrange("p b (t c) -> p (b t) c", c=SW)
                return lambda t: v[:, t, :]

            hT = (hTH, hTL)
            both = pair_cols()

            def all_cols(t, k):
                return t[:, k, :]

            g = product_at["setup"]
            pe.wait_ge(s_setup, 7 * 16)
            pe.transpose(G[0][:, 0, 0:61], gainRows[0:61, :], ident[0:61, 0:61])
            pe.transpose(G[0][:, 0, 64:128], posRows[:, :], ident[0:64, 0:64])
            pe.matmul(G[0][0:16, 1, :], tab[:, :], onehot[:, :], start=True, stop=True).then_inc(product_ready, 1)
            for i in range(4):
                g = product_at["x", i]
                free(g)
                for b in range(2):
                    for t in range(NT):
                        pe.wait_ge(x_scaled, t + 1)
                        mm = pe.transpose(G[g % 2][:, b, t * P:(t + 1) * P], xN[:, t, (2 * i + b) * P:(2 * i + b + 1) * P], ident[:, :])
                mm.then_inc(product_ready, 1)
            pe.wait_ge(taken["V"], taken_count[product_at["x", 3]])
            for i in range(2):
                g, s = product_at["lat", i], slab_at["lat", i]
                free(g)
                n_mode(s, tokens_out(g), all_cols, KD, hT).then_inc(product_ready, 1)
            g, s = product_at["lat", 2], slab_at["lat", 2]
            free(g)
            v = tokens_out(g)
            n_mode(s, lambda t: v(t)[:, 0:P + 32], lambda t, k: t[:, k, 0:P + 32], KD, hT).then_inc(product_ready, 1)
            g = product_at["krope"]
            free(g)
            t_mode(slab_at["kr",], two(g), both, KD, hT).then_inc(product_ready, 1)
            for i in range(2):
                g = product_at["iq", i]
                free(g)
                t_mode(slab_at["iq", i], two(g), both, KD, hT).then_inc(product_ready, 1)
            g, s = product_at["ik"], slab_at["ik",]
            free(g)
            t_mode(s, two(g)[0:1], pair_cols(0)[0:1], KD, hT).then_inc(product_ready, 1)
            pe.wait_ge(lat_scaled, NT)
            for i in range(3):
                g = product_at["latT", i]
                free(g)
                for b in range(2 if i < 2 else 1):
                    for t in range(NT):
                        c = (2 * i + b) * P
                        mm = pe.transpose(G[g % 2][:, b, t * P:(t + 1) * P], latN[:, t, c:c + P], ident[:, :])
                mm.then_inc(product_ready, 1)
            pe.wait_ge(taken["A"], taken_count[product_at["iq", 0]])
            pe.wait_ge(taken["V"], taken_count[product_at["ik"]])
            n = 0
            for i in range(1, NT):
                for h in range(8):
                    if n >= 2:
                        pe.wait_ge(index_taken, n - 1)
                    r = slice(64 * (h % 2), 64 * (h % 2) + 64)
                    pe.matmul(S[n % 2][:, 0:(i + 1) * P], iqT[r, h // 2, i * P:(i + 1) * P],
                              ikT[r, 0:(i + 1) * P], start=True, stop=True).then_inc(index_ready, 1)
                    n += 1
            pe.wait_ge(index_taken, INDEX_TILES)

            def score_tile(n, terms, cols):
                if n >= 3:
                    pe.wait_ge(score_taken, n - 2)
                for j, (q, k) in enumerate(terms):
                    mm = pe.matmul(SCORE[n % 3][:, 0:cols], q, k, start=j == 0, stop=j == len(terms) - 1)
                mm.then_inc(score_ready, 1)

            def attend(heads, m):
                def turn_tile(unit, probs_of, i0, rows, m):
                    pe.wait_ge(probs_ready, unit + 1)
                    if m > 1:
                        pe.wait_ge(probsT_ready, m - 1)
                    for i in range(i0, NT):
                        mm = pe.transpose(TURNED[m % 2][0:rows, (i - i0) * P:(i - i0 + 1) * P], probs_of(i), ident[:, :])
                    mm.then_inc(turned_ready, 1)

                def value_tile(att, first, last, value, i0, rows, m):
                    pe.wait_ge(probsT_ready, m + 1)
                    if first and att > 1:
                        pe.wait_ge(attended_taken, att - 1)
                    mm = pe.matmul(ATT[att % 2][:, i0 * P:T], value, probsT[0:rows, m % 3, 0:T - i0 * P],
                                   start=first, stop=last)
                    if last:
                        mm.then_inc(attended_ready, 1)

                late_one = None
                for att, parts in heads:
                    for n, (unit, probs_of, i0, rows, value) in enumerate(parts):
                        turn_tile(unit, probs_of, i0, rows, m)
                        if late_one:
                            value_tile(*late_one)
                        late_one = (att, n == 0, n == len(parts) - 1, value, i0, rows, m)
                        m += 1
                value_tile(*late_one)

            def causal_parts(unit, slot, value_of):
                def block(j):
                    return lambda i: probs[:, slot, TRI[i] + j * P:TRI[i] + (j + 1) * P]
                return [(unit, block(j), j, P, value_of(j)) for j in range(NT)]

            lat = (latH, latL)

            def uq_cols(c):
                return lambda t, k: wide(t, 3, 512)[:, k, c:c + P]

            def mla_values(p):
                attend([(2 * p + h, causal_parts(2 * p + h, h, lambda j, h=h: vN[:, j, h * P:(h + 1) * P]))
                        for h in range(2)], 8 * p)

            def mla_v(p):
                s = slab_at["ukv", p]
                g = product_at["m4", p]
                free(g)
                v = G[g % 2][:, :, :].rearrange("p b (t h c) -> p (b t) h c", h=2, c=P)
                n_mode(s, lambda t: v[:, t, :, :],
                       lambda t, k: wide(t, 2, 512)[:, k, :].rearrange("p (h c) -> p h c", c=256)[:, :, P:2 * P],
                       2, (latH[:, 3:5, :], latL[:, 3:5, :])).then_inc(product_ready, 1)

            for p in range(4):
                s = slab_at["uq", p]
                g = product_at["m1", p]
                free(g)
                if p == 0:
                    pe.wait_ge(taken["V"], taken_count[product_at["latT", 2]])
                t_mode(s, two(g), [uq_cols(0), uq_cols(128)], 3, lat).then_inc(product_ready, 1)
                g = product_at["m2", p]
                free(g)
                t_mode(s, two(g), [uq_cols(256), uq_cols(384)], 3, lat).then_inc(product_ready, 1)
                s = slab_at["ukv", p]
                g = product_at["m3", p]
                free(g)
                t_mode(s, two(g), [lambda t, k: wide(t, 2, 512)[:, k, 0:P], lambda t, k: wide(t, 2, 512)[:, k, 256:384]],
                       2, (latH[:, 3:5, :], latL[:, 3:5, :])).then_inc(product_ready, 1)
                if p:
                    mla_values(p - 1)
                else:
                    mla_v(p)
                pe.wait_ge(taken["V"], taken_count[product_at["m2", p]])
                pe.wait_ge(taken["A"], taken_count[product_at["m3", p]])
                if p:
                    pe.wait_ge(attended_taken, 2 * p - 1)
                for h in range(2):
                    r = slice(64 * h, 64 * h + 64)
                    for i in range(NT):
                        q = slice(i * P, (i + 1) * P)
                        score_tile((2 * p + h) * NT + i, [(qT[:, h, q], kT[:, h, 0:(i + 1) * P]),
                                                          (qrT[r, q], krT[r, 0:(i + 1) * P])], (i + 1) * P)
                if p:
                    mla_v(p)
            pe.wait_ge(taken["A"], taken_count[product_at["m4", 3]])

            def merge(b, last_values):
                for n in range(GROUPS):
                    g = product_at["bg", b, n]
                    free(g)
                    t_mode(slab_at["bg", b, n], two(g), both, KD, hT).then_inc(product_ready, 1)
                    if n == 0:
                        last_values()
                    g = product_at["bp", b, n]
                    free(g)
                    t_mode(slab_at["bp", b, n], two(g), both, KD, (oTH, oTL),
                           lambda k: pe.wait_ge(attended_taken, 8 * b + k + 1)).then_inc(product_ready, 1)

            merge(0, lambda: mla_values(3))

            def dsa_values(p):
                attend([(8 + 2 * p + h, causal_parts(8 + 2 * p + h, h, lambda j, h=h: vN[:, j, h * P:(h + 1) * P]))
                        for h in range(2)], 32 + 8 * p)

            def dsa_v(p):
                g = product_at["dv", p]
                free(g)
                n_mode(slab_at["dv", p], tokens_out(g), all_cols, KD, hT).then_inc(product_ready, 1)

            for p in range(4):
                for name in ("dq", "dk"):
                    g = product_at[name, p]
                    free(g)
                    t_mode(slab_at[name, p], two(g), both, KD, hT).then_inc(product_ready, 1)
                if p:
                    dsa_values(p - 1)
                else:
                    dsa_v(0)
                pe.wait_ge(taken["A"], taken_count[product_at["dq", p]])
                pe.wait_ge(taken["V"], taken_count[product_at["dk", p]])
                if p:
                    pe.wait_ge(attended_taken, 8 + 2 * p - 1)
                for h in range(2):
                    for i in range(NT):
                        score_tile((8 + 2 * p + h) * NT + i, [(qT[:, h, i * P:(i + 1) * P], kT[:, h, 0:(i + 1) * P])], (i + 1) * P)
                if p:
                    dsa_v(p)
            pe.wait_ge(taken["A"], taken_count[product_at["dv", 3]])
            merge(1, lambda: dsa_values(3))

            for name in ("kc", "vc"):
                g = product_at[name]
                free(g)
                t_mode(slab_at[name,], two(g), both, KD, hT).then_inc(product_ready, 1)

            def hidden_rows(kv, c):
                s = slab_at["cw", kv, c]
                if c == 0:
                    pe.wait_ge(flat_split, kv + 1)
                slab_half(s, 0)
                for k in range(KD):
                    if k == KD // 2:
                        slab_half(s, 1)
                    l = (c * KD + k) * 2 * NC
                    mm = blocks3(S[kv][:, 0:SW], (flatH[kv][:, l:l + P], flatL[kv][:, l:l + P]),
                                 (wh[s % 2][:, k, :], wl[s % 2][:, k, :]), c + k == 0, c == 3 and k == KD - 1)
                mm.then_inc(product_ready, 1)

            def turn_hidden():
                g = product_at["hidT"]
                free(g)
                pe.wait_ge(hid_taken, 2)
                for kv in range(2):
                    for k in range(2):
                        col = (2 * kv + k) * 2 * NC
                        mm = pe.transpose(G[g % 2][:, 0, col:col + 2 * NC], hidR[:, kv, k * P:(k + 1) * P],
                                          ident[0:2 * NC, 0:2 * NC])
                mm.then_inc(product_ready, 1)

            def compress():
                g = product_at["cmp"]
                free(g)
                pe.wait_ge(cmp2_loaded, 32)
                pe.wait_ge(taken["V"], taken_count[product_at["hidT"]])
                for k in range(2):
                    pe.matmul(G[g % 2][:, 0, 0:2 * NC], cmpW2[:, 0, k, :], hid[:, 0, k, :], start=k == 0, stop=k == 1)
                for r in range(2):
                    for k in range(2):
                        mm = pe.matmul(G[g % 2][0:NC, 1, r * P:(r + 1) * P], hid[:, 1, k, r * NC:(r + 1) * NC], cmpW2[:, 1, k, :],
                                       start=k == 0, stop=k == 1)
                mm.then_inc(product_ready, 1)

            def nsa_values(p):
                heads = []
                for h in range(2):
                    parts = []
                    for w in range(2):
                        parts += causal_parts(16 + 6 * p + 2 * h + w, 2 * h + w, lambda j, w=w: vN[:, j, w * P:(w + 1) * P])
                    parts.append((16 + 6 * p + 4 + h, lambda i, h=h: probC[:, h, i, 0:NC], 0, NC, vcmp[0:NC, p // 2, :]))
                    heads.append((16 + 2 * p + h, parts))
                attend(heads, 64 + 18 * p)

            def features(name, i):
                g = product_at[name, i]
                free(g)
                t_mode(slab_at[name, i], two(g), both, KD, hT).then_inc(product_ready, 1)

            def nsa_v(r):
                g = product_at["vv", r]
                free(g)
                n_mode(slab_at["vv", r], tokens_out(g), all_cols, KD, hT).then_inc(product_ready, 1)

            for name, i in NSA_BEGIN:
                if name == "cw":
                    hidden_rows(*i)
                elif name == "vv":
                    nsa_v(i)
                else:
                    features(name, i)
            turn_hidden()
            compress()
            for p in range(4):
                r = p // 2
                if p:
                    features("nq", p)
                    if p == 2:
                        features("kk", r)
                    nsa_values(p - 1)
                    if p == 2:
                        nsa_v(r)
                pe.wait_ge(taken["A"], taken_count[product_at["nq", p]])
                pe.wait_ge(taken["V"], taken_count[product_at["kk", r] if r else product_at["cmp"]])
                if p:
                    pe.wait_ge(attended_taken, 16 + 2 * p - 1)
                n = TILE_NSA + NSA_TILES * p
                for h in range(2):
                    for w in range(2):
                        for i in range(NT):
                            score_tile(n, [(qT[:, h, i * P:(i + 1) * P], kT[:, w, 0:(i + 1) * P])], (i + 1) * P)
                            n += 1
                for h in range(2):
                    pe.wait_ge(score_taken, n - 2)
                    for i in range(NT):
                        mm = pe.matmul(SCORE[n % 3][:, i * 32:i * 32 + NC], qT[:, h, i * P:(i + 1) * P],
                                       kcmpT[:, r * NC:(r + 1) * NC], start=True, stop=True)
                    mm.then_inc(score_ready, 1)
                    n += 1
                if p % 2 == 0:
                    pe.wait_ge(taken["A"], taken_count[product_at["vv", r]])
            merge(2, lambda: nsa_values(3))

            pe.wait_ge(x2_loaded, 16)

            def turn_residual(i):
                g = product_at["xt", i]
                free(g)
                for b in range(2):
                    for t in range(NT):
                        mm = pe.transpose(G[g % 2][:, b, t * P:(t + 1) * P], xN2[:, t, (2 * i + b) * P:(2 * i + b + 1) * P], ident[:, :])
                mm.then_inc(product_ready, 1)

            def turn_memory(i):
                pe.wait_ge(mem_scaled, 2)
                if i:
                    pe.wait_ge(mem_taken, i)
                for c in range(4):
                    for t in range(2):
                        col = c % 2 * MEM + t * P
                        mm = pe.transpose(S[c // 2][:, col:col + P], memN[:, t, (4 * i + c) * P:(4 * i + c + 1) * P], ident[:, :])
                mm.then_inc(mem_turned, 1)

            def wait_count(sem_, per=1):
                return lambda k: pe.wait_ge(sem_, k + 1)

            def post_squares(j, last_squares):
                if j == 0:
                    pe.wait_ge(ones_ready, 1)
                pe.wait_ge(squares_added, (GROUPS - 1) * (j + 1))
                pe.matmul(PT[:, :], ones[:, :], squareSum[:, :], start=True, stop=False)
                pe.wait_ge(*last_squares)
                for b in range(2):
                    mm = pe.matmul(PT[:, :], ones[:, :], outSquare[j][:, (GROUPS - 1) % 2, b, :], start=False, stop=b == 1)
                mm.then_inc(post_sum[j], 1)

            def out_projection(j, name, act, wait_chunk, begun=0):
                for n in range(GROUPS):
                    if name == "wo" and n < 2:
                        turn_residual(2 * n)
                        turn_residual(2 * n + 1)
                    elif name == "wo":
                        turn_memory(n - 2)
                    g = product_at[name, n]
                    free(g)
                    k0 = begun if n < 2 else 0
                    t_mode(slab_at[name, n], two(g), both, KD - k0, act, (lambda k: wait_chunk(k0 + k)) if n == 0 else None,
                           k0, KD, k0).then_inc(product_ready, 1)
                post_squares(j, (squared, GROUPS * (j + 1)))

            def pre_squares(j):
                for c in range(KD):
                    pe.wait_ge(presq_ready[j], c + 1)
                    pe.matmul(OT[:, :], ones[:, :], square[:, c // 2 % 2, c % 2, :], start=c == 0,
                              stop=c == KD - 1).then_inc(presum[j], 1)

            out_projection(0, "wo", (mgH, mgL), lambda k: pe.wait_ge(merged_ready, k // 2 + 1))
            pe.wait_ge(mem_taken, 2)
            mem = (memH, memL)
            for n in range(GROUPS):
                if n == 2:
                    pre_squares(0)
                g = product_at["ck", n]
                free(g)
                t_mode(slab_at["ck", n], [G[g % 2][:, b, 0:MEM] for b in range(2)], both, KD, mem).then_inc(product_ready, 1)
            for n in range(GROUPS):
                g = product_at["cv", n]
                free(g)
                n_mode(slab_at["cv", n], lambda t: G[g % 2][:, t, 0:SW], all_cols, KD, mem, tiles=2).then_inc(product_ready, 1)

            def cross_values(n):
                pe.wait_ge(cprobs_ready, n + 1)
                pe.wait_ge(cross_taken, (n + 1) * NT)
                for j in range(2):
                    if n:
                        pe.wait_ge(cprobsT_ready, 2 * n)
                    for i in range(NT):
                        mm = pe.transpose((PT, S[0])[j][:, i * P:(i + 1) * P], probX[:, i, j * P:(j + 1) * P], ident[:, :])
                    mm.then_inc(cturned_ready, 1)
                if n:
                    pe.wait_ge(catt_taken, 2 * n)
                for b in range(2):
                    for j in range(2):
                        pe.wait_ge(cprobsT_ready, 2 * n + j + 1)
                        mm = pe.matmul((OT, S[1])[b][:, :], vxN[:, j, n * SW + b * P:n * SW + (b + 1) * P], probXT[:, j, :],
                                       start=j == 0, stop=j == 1)
                    mm.then_inc(catt_ready, 1)

            for n in range(GROUPS):
                g = product_at["cq", n]
                free(g)
                t_mode(slab_at["cq", n], two(g), both, KD, hT, wait_count(nhid_ready[0]) if n == 0 else None).then_inc(product_ready, 1)
                if n:
                    cross_values(n - 1)
                pe.wait_ge(taken["A"], taken_count[g])
                for i in range(NT):
                    m = n * NT + i
                    if i >= 2:
                        pe.wait_ge(cross_taken, m - 1)
                    if n and i == 1:
                        pe.wait_ge(catt_taken, 2 * n)
                    for b in range(2):
                        mm = pe.matmul(S[m % 2][:, 0:MEM], qT[:, b, i * P:(i + 1) * P], kxT[:, 2 * n + b, :], start=b == 0, stop=b == 1)
                    mm.then_inc(cross_ready, 1)
            for n in range(2):
                g = product_at["co", n]
                free(g)
                t_mode(slab_at["co", n], two(g), both, 6, (coH, coL), lambda k: pe.wait_ge(catt_taken, k + 1), 0, KD)
            cross_values(3)
            out_projection(1, "co", (coH, coL), lambda k: pe.wait_ge(catt_taken, k + 1), 6)
            pre_squares(1)

            up = (h1H, h1L)
            for f in range(2):
                for n in range(8):
                    g = product_at["up", f, n]
                    free(g)
                    t_mode(slab_at["up", f, n], two(g), both, KD, hT,
                           wait_count(nhid_ready[1]) if f == 0 and n == 0 else None).then_inc(product_ready, 1)
                for n in range(GROUPS):
                    g = product_at["down", f, n]
                    free(g)
                    for k in range(2):
                        t_mode(slab_at["down", f, n, k], two(g), both, KD, up,
                               lambda c, k=k: pe.wait_ge(up_ready, 8 * f + (k * KD + c) // 2 + 1), k * KD, 16).then_inc(product_ready, 1)
            post_squares(2, (downsq_ready, GROUPS))
            for i in range(4):
                g = product_at["out", i]
                free(g)
                v = tokens_out(g)
                pe.wait_ge(resid_ready[2], i + 1)
                pe.wait_ge(resid_dve[2], i + 1)
                for c in range(2):
                    for t in range(NT):
                        mm = pe.transpose(v(t)[:, c * P:(c + 1) * P], XT[:, 2 * i + c, t * P:(t + 1) * P], ident[:, :])
                mm.then_inc(product_ready, 1)

        @block.scalar
        def _(act):
            roots = [0]

            def ready(name):
                act.wait_ge(product_ready, ready_at[name])

            def copy(dst, src, scale=1.0):
                return nc.scalar.activation(dst, src, ACT.Copy, scale=scale)

            def high(s):
                if s >= SLABS:
                    return
                act.wait_ge(loaded[s % 2], landed[s])
                if s >= 2:
                    act.wait_ge(product_ready, used_at[s - 2])
                if s in halved:
                    for dst, src in half_pieces(s, wh[s % 2], raw[s % 2]):
                        copy(dst, src).then_inc(high_ready, 1)
                    return
                for dst, src in split_pieces(s, wh[s % 2], raw[s % 2]):
                    ins = copy(dst, src)
                ins.then_inc(high_ready, 1)

            def bank(name):
                return G[product_at[name] % 2]

            def root(tile):
                nc.scalar.activation(tile, tile, ACT.Sqrt).then_inc(root_done, 1)
                roots[0] += 1

            junk = vN[:, :, :].rearrange("p t c -> p (t c)")

            def x_root(t):
                act.wait_ge(xroot_ready, t + 1)
                root(nstat[:, t:t + 1])

            for t in range(NT):
                act.wait_ge(s_x[t], 16)
                if t:
                    act.wait_ge(xsum_ready, t)
                nc.scalar.activation(junk, xN[:, t, :], ACT.Square, accum_out=stat[:, t:t + 1]).then_inc(xsum_ready, 1)
                if t:
                    x_root(t - 1)
            x_root(NT - 1)
            act.wait_ge(taken["V"], 1)
            for i in range(4):
                ready(("x", i))
                for b in range(2):
                    c = 2 * i + b
                    ins = copy(hTH[:, c, :], bank(("x", i))[:, b, :], gains[:, c:c + 1])
                ins.then_inc(hidden_high, 1)
                if i % 2:
                    high(i // 2)
            act.wait_ge(angle_ready, 1)
            nc.scalar.activation(sinT[:, :], sinT[:, :], ACT.Sin)
            nc.scalar.activation(cosT[:, :], cosT[:, :], ACT.Sin).then_inc(sine_ready, 1)

            for i in range(2):
                ready(("lat", i))
                copy(latN[:, :, i * SW:(i + 1) * SW], bank(("lat", i))[:, :, :].rearrange("p b (t c) -> p (b t) c", c=SW)).then_inc(taken["A"], 1)
                high(i + 2)
            ready(("lat", 2))
            v = bank(("lat", 2))[:, :, :].rearrange("p b (t c) -> p (b t) c", c=SW)
            copy(iw, v[:, :, P:P + 8])
            copy(gateN[:, :, :], v[:, :, P + 8:P + 32])
            copy(latN[:, :, 512:640], v[:, :, 0:P]).then_inc(taken["A"], 1)
            high(slab_at["lat", 2] + 2)
            act.wait_ge(taken["A"], 3)
            for t in range(NT):
                if t:
                    act.wait_ge(latsum_ready, t)
                nc.scalar.activation(junk[:, 0:DQ], latN[:, t, 0:DQ], ACT.Square, accum_out=stat[:, t:t + 1])
                nc.scalar.activation(junk[:, DQ:DQ + DKV], latN[:, t, DQ:DQ + DKV], ACT.Square,
                                     accum_out=stat[:, 4 + t:5 + t]).then_inc(latsum_ready, 1)
            act.wait_ge(latsum_ready, NT + 1)
            root(nstat[:, 0:8])
            high(slab_at["kr",] + 2)
            ready(("iq", 0))
            copy(iqT[:, 0:2, :], bank(("iq", 0))[:, :, :]).then_inc(taken["A"], 1)
            high(slab_at["iq", 0] + 2)
            high(slab_at["iq", 1] + 2)
            high(slab_at["ik",] + 2)
            for i in range(3):
                ready(("latT", i))
                for b in range(2 if i < 2 else 1):
                    c = 2 * i + b
                    ins = copy(latH[:, c, :], bank(("latT", i))[:, b, :], gains[:, 56 + c:57 + c])
                ins.then_inc(lat_high, 1)
            n = 0
            for i in range(1, NT):
                for h in range(8):
                    act.wait_ge(index_ready, n + 1)
                    if n >= 2:
                        act.wait_ge(index_added, n - 1)
                    nc.scalar.activation(relu[:, n % 2, 0:(i + 1) * P], S[n % 2][:, 0:(i + 1) * P], ACT.Relu).then_inc(index_taken, 1)
                    n += 1

            def exps(u, slot):
                act.wait_ge(negmax_ready, u + 1)
                for i in range(NT):
                    t = probs[:, slot, TRI[i]:TRI[i] + (i + 1) * P]
                    k = 4 * slot + i
                    ins = nc.scalar.activation(t, t, ACT.Exp, bias=negmax[:, k:k + 1], accum_out=total[:, k:k + 1])
                ins.then_inc(exp_done, 1)

            def turned(heads, m):
                def head_out(att):
                    act.wait_ge(attended_ready, att + 1)
                    copy(oTH[:, att % 8, :], ATT[att % 2][:, :]).then_inc(attended_high, 1)

                waiting = None
                for att, tiles in heads:
                    for n, (rows, cols) in enumerate(tiles):
                        act.wait_ge(turned_ready, m + 1)
                        copy(probsT[0:rows, m % 3, 0:cols], TURNED[m % 2][0:rows, 0:cols]).then_inc(probsT_ready, 1)
                        m += 1
                        if n == 0 and waiting is not None:
                            head_out(waiting)
                    waiting = att
                head_out(waiting)

            causal = [(P, T - j * P) for j in range(NT)]
            act.wait_ge(scratch_written, 16)
            for p in range(4):
                s = slab_at["uq", p]
                ready(("m1", p))
                copy(qT[:, :, :], bank(("m1", p))[:, :, :]).then_inc(taken["A"], 1)
                ready(("m2", p))
                high(s + 2)
                ready(("m3", p))
                copy(kT[:, :, :], bank(("m3", p))[:, :, :]).then_inc(taken["A"], 1)
                if p:
                    turned([(2 * (p - 1) + h, causal) for h in range(2)], 8 * (p - 1))
                for h in range(2):
                    if p:
                        exps(2 * p + h, h)
                ready(("m4", p))
                copy(vN[:, :, :], bank(("m4", p))[:, :, :].rearrange("p b (t c) -> p (b t) c", c=SW)).then_inc(taken["A"], 1)
                high(s + 3)
                for h in range(2):
                    if not p:
                        exps(2 * p + h, h)

            def merge(b, tiles, first_tile):
                for n in range(GROUPS):
                    ready(("bg", b, n))
                    if n or b:
                        last = product_at["bp", b, n - 1] if n else product_at["bp", b - 1, GROUPS - 1]
                        act.wait_ge(taken["V"], taken_count[last])
                    nc.scalar.activation(sig[:, :, :], bank(("bg", b, n))[:, :, :], ACT.Sigmoid).then_inc(taken["A"], 1)
                    if n == 0:
                        turned([(8 * b + 6 + h, tiles) for h in range(2)], first_tile)
                    high(slab_at["bg", b, n] + 2)
                    if b == 2 and n:
                        merged_split(n - 1)
                    high(slab_at["bp", b, n] + 2)

            def merged_split(n):
                act.wait_ge(merge_added, GROUPS + n + 1)
                copy(mgH[:, 2 * n:2 * n + 2, :], merged[:, 2 * n:2 * n + 2, :]).then_inc(merged_high, 1)

            merge(0, causal, 24)
            for p in range(4):
                ready(("dq", p))
                if p == 0:
                    act.wait_ge(taken["V"], taken_count[product_at["bp", 0, GROUPS - 1]])
                copy(qT[:, :, :], bank(("dq", p))[:, :, :], HEAD_SCALE).then_inc(taken["A"], 1)
                high(slab_at["dq", p] + 2)
                if p:
                    turned([(8 + 2 * (p - 1) + h, causal) for h in range(2)], 32 + 8 * (p - 1))
                high(slab_at["dk", p] + 2)
                for h in range(2):
                    if p:
                        exps(8 + 2 * p + h, h)
                ready(("dv", p))
                copy(vN[:, :, :], bank(("dv", p))[:, :, :].rearrange("p b (t c) -> p (b t) c", c=SW)).then_inc(taken["A"], 1)
                high(slab_at["dv", p] + 2)
                for h in range(2):
                    if not p:
                        exps(8 + 2 * p + h, h)
            merge(1, causal, 56)

            act.wait_ge(taken["V"], taken_count[product_at["bp", 1, GROUPS - 1]])
            act.wait_ge(merge_added, GROUPS)
            def flat_split_high(kv):
                act.wait_ge(flat_ready, kv + 1)
                v = flatH[kv][:, 0:FLAT].rearrange("p (l c) -> p l c", c=2 * NC)
                for r in range(2):
                    ins = copy(v[:, :, r * NC:(r + 1) * NC], flat_[:, r, :, :])
                ins.then_inc(flat_high, 1)

            for kv, (name, dst) in enumerate((("kc", kcT), ("vc", vcT))):
                ready(name)
                copy(dst[:, :, :], bank(name)[:, :, :]).then_inc(taken["A"], 1)
                if kv == 0:
                    high(slab_at[name,] + 2)
                flat_split_high(kv)
                if kv:
                    high(slab_at[name,] + 2)
            nc.scalar.activation(gateN[:, :, :], gateN[:, :, :], ACT.Sigmoid).then_inc(gates_ready, 1)

            def nsa_query(p):
                ready(("nq", p))
                copy(qT[:, :, :], bank(("nq", p))[:, :, :], HEAD_SCALE).then_inc(taken["A"], 1)

            def nsa_value(r):
                ready(("vv", r))
                copy(vN[:, :, :], bank(("vv", r))[:, :, :].rearrange("p b (t c) -> p (b t) c", c=SW)).then_inc(taken["A"], 1)

            for name, i in NSA_BEGIN:
                if name == "nq":
                    nsa_query(i)
                if name == "vv":
                    act.wait_ge(flat_split, 2)
                    nsa_value(i)
                if name == "cw" and i[1] == 3:
                    ready(("hid", i[0]))
                    nc.scalar.activation(hidR[:, i[0], :], S[i[0]][0:2 * NC, 0:SW], ACT.Gelu_apprx_tanh).then_inc(hid_taken, 1)
                high(slab_at[(name, *i) if name == "cw" else (name, i)] + 2)
            nsa = 2 * causal + [(NC, T)]
            for p in range(4):
                r = p // 2
                if p:
                    nsa_query(p)
                    if p == 2:
                        high(slab_at["nq", p] + 2)
                    turned([(16 + 2 * (p - 1) + h, nsa) for h in range(2)], 64 + 18 * (p - 1))
                    high(slab_at["kk", r] + 2 if p == 2 else slab_at["nq", p] + 2)
                if p == 2:
                    nsa_value(r)
                    high(slab_at["vv", r] + 2)
                for u in range(4):
                    exps(16 + 4 * p + u, u)
                for h in range(2):
                    act.wait_ge(cmpmax_ready, 2 * p + h + 1)
                    t = probC[:, h, :, 0:NC]
                    nc.scalar.activation(t, t, ACT.Exp).then_inc(cmpexp_done, 1)
            merge(2, nsa, 64 + 54)

            def post(j):
                act.wait_ge(post_sum[j], 1)
                nc.scalar.activation(rstd[:, :], PT[:, :], ACT.Sqrt, bias=eps, scale=1.0 / D).then_inc(rms_ready, 1)

            def projection(name, n):
                j = ("wo", "co").index(name)
                ready((name, n))
                g = bank((name, n))
                if n > 1:
                    act.wait_ge(squares_added, (GROUPS - 1) * j + n - 1)
                nc.scalar.activation(outSquare[j][:, n % 2, :, :], g[:, :, :], ACT.Square).then_inc(squared, 1)
                copy(yT[:, 2 * n:2 * n + 2, :], g[:, :, :]).then_inc(taken["A"], 1)
                if name == "co" and n == GROUPS - 1:
                    post(1)
                high(slab_at[name, n] + 2)

            def pre_squared(j):
                for c in range(KD):
                    if j == 0:
                        act.wait_ge(resid_ready[j], c + 1)
                    else:
                        act.wait_ge((resid_ready, resid_dve)[c % 2][j], c // 2 + 1)
                    if c >= 4:
                        act.wait_ge(presum[j], c - 3)
                    nc.scalar.activation(square[:, c // 2 % 2, c % 2, :], XT[:, c, :], ACT.Square).then_inc(presq_ready[j], 1)

            def cross_value_rows(n):
                ready(("cv", n))
                copy(vxN[:, :, n * SW:(n + 1) * SW], bank(("cv", n))[:, :, 0:SW]).then_inc(taken["A"], 1)
                high(slab_at["cv", n] + 2)

            def pre(j):
                act.wait_ge(presum[j], KD)
                nc.scalar.activation(rstd[:, :], OT[:, :], ACT.Sqrt, bias=eps, scale=1.0 / D).then_inc(rms_ready, 1)
                for c in range(KD):
                    if j == 0 and c in (2, 4):
                        high(slab_at["ck", 1 + c // 2] + 2)
                    if j == 0 and c == 6:
                        cross_value_rows(0)
                    act.wait_ge(normed_ready[j], c + 1)
                    copy(hTH[:, c, :], normed[:, c % 2, :]).then_inc(nhigh_ready[j], 1)

            for n in range(2):
                ready(("xt", 2 * n))
                copy(XT[:, 4 * n:4 * n + 2, :], bank(("xt", 2 * n))[:, :, :]).then_inc(taken["A"], 1)
                if n == 0:
                    merged_split(GROUPS - 1)
                    projection("wo", 0)
            act.wait_ge(mem_loaded, 16)
            ready(("xt", 3))
            for t in range(2):
                if t:
                    act.wait_ge(memsum_ready, t)
                nc.scalar.activation(normed[:, :, :].rearrange("p b c -> p (b c)"), memN[:, t, :], ACT.Square,
                                     accum_out=stat[:, t:t + 1]).then_inc(memsum_ready, 1)
            act.wait_ge(memroot_ready, 1)
            root(nstat[:, 0:2])
            for i in range(2):
                projection("wo", i + 1)
                act.wait_ge(mem_turned, i + 1)
                for c in range(4):
                    k = 4 * i + c
                    ins = copy(memH[:, k, :], S[c // 2][:, c % 2 * MEM:(c % 2 + 1) * MEM], gains[:, 24 + k:25 + k])
                ins.then_inc(mem_high, 1)
            projection("wo", GROUPS - 1)
            post(0)
            high(slab_at["ck", 0] + 2)
            pre_squared(0)
            high(slab_at["ck", 1] + 2)
            pre(0)
            for n in range(1, GROUPS):
                cross_value_rows(n)

            def cross_turned(n):
                for j in range(2):
                    m = 2 * n + j
                    act.wait_ge(cturned_ready, m + 1)
                    copy(probXT[:, j, :], (PT, S[0])[j][:, :]).then_inc(cprobsT_ready, 1)
                for b in range(2):
                    act.wait_ge(catt_ready, 2 * n + b + 1)
                    copy(coH[:, 2 * n + b, :], (OT, S[1])[b][:, :]).then_inc(catt_high, 1)

            for n in range(GROUPS):
                ready(("cq", n))
                copy(qT[:, :, :], bank(("cq", n))[:, :, :], CROSS_SCALE).then_inc(taken["A"], 1)
                if n:
                    cross_turned(n - 1)
                for i in range(NT):
                    m = n * NT + i
                    act.wait_ge(cmax_ready, m + 1)
                    nc.scalar.activation(probX[:, i, :], S[m % 2][:, 0:MEM], ACT.Exp, bias=negmax[:, i:i + 1],
                                         accum_out=total[:, i:i + 1]).then_inc(cross_taken, 1)
                high(slab_at["cq", n] + 2)
            cross_turned(3)
            nc.scalar.activation(spare, eps, ACT.Sqrt)
            for n in range(GROUPS):
                projection("co", n)
            pre_squared(1)
            pre(1)

            def up_split(n):
                act.wait_ge(up_squared, n + 1)
                copy(h1H[:, 2 * (n % 8):2 * (n % 8) + 2, :], h1[:, n % 2, :, :]).then_inc(up_high, 1)

            for f in range(2):
                for n in range(8):
                    ready(("up", f, n))
                    u = 8 * f + n
                    if u >= 2:
                        act.wait_ge(up_ready, u - 1)
                    nc.scalar.activation(h1[:, n % 2, :, :], bank(("up", f, n))[:, :, :], ACT.Relu).then_inc(taken["A"], 1)
                    high(slab_at["up", f, n] + 2)
                    if n:
                        up_split(u - 1)
                up_split(8 * f + 7)
                for n in range(GROUPS):
                    s = slab_at["down", f, n, 0]
                    high(s + 2)
                    if f == 0:
                        ready(("down", f, n))
                        copy(yT[:, 2 * n:2 * n + 2, :], bank(("down", f, n))[:, :, :]).then_inc(taken["A"], 1)
                    else:
                        act.wait_ge(taken["V"], taken_count[product_at["down", f, n]])
                        if n > 1:
                            act.wait_ge(squares_added, (GROUPS - 1) * 2 + n - 1)
                        nc.scalar.activation(square[:, n % 2, :, :], yT[:, 2 * n:2 * n + 2, :], ACT.Square).then_inc(downsq_ready, 1)
                    high(s + 3)
            post(2)
            for i in range(4):
                ready(("out", i))
                copy(outN[:, :, i * SW:(i + 1) * SW], bank(("out", i))[:, :, :].rearrange("p b (t c) -> p (b t) c", c=SW)).then_inc(taken["A"], 1)

        @block.vector
        def _(dve):
            steps = [0]
            V = nc.vector

            def link(ins):
                steps[0] += 1
                ins.then_inc(dve_step, 1)
                dve.wait_ge(dve_step, steps[0])

            def ready(name):
                dve.wait_ge(product_ready, ready_at[name])

            def bank(name):
                return G[product_at[name] % 2]

            def low(s):
                if s >= SLABS:
                    return
                if s in halved:
                    halves = zip(half_pieces(s, wl[s % 2], raw[s % 2]), half_pieces(s, wh[s % 2], raw[s % 2]))
                    for n, ((dst, src), (hi, _)) in enumerate(halves):
                        dve.wait_ge(high_ready, split_at[s] - 1 + n)
                        V.tensor_tensor(dst, src, hi.bitcast(F32), ALU.subtract).then_inc(low_ready, 1)
                    return
                dve.wait_ge(high_ready, split_at[s])
                pieces = zip(split_pieces(s, wl[s % 2], raw[s % 2]), split_pieces(s, wh[s % 2], raw[s % 2]))
                for (dst, src), (hi, _) in pieces:
                    ins = V.tensor_tensor(dst, src, hi.bitcast(F32), ALU.subtract)
                ins.then_inc(low_ready, 1)

            def rest(dst, src, hi, gain):
                return V.scalar_tensor_tensor(dst, src, gain, hi.bitcast(F32), ALU.mult, ALU.subtract)

            def root_arg(dst, src, width):
                return V.tensor_scalar(dst, src, 1.0 / width, EPS, ALU.mult, ALU.add)

            V.memset(biasRow[:, T:], NEG)
            V.memset(eps, EPS)

            def x_scale(t):
                dve.wait_ge(root_done, t + 1)
                link(V.reciprocal(rstat[:, t:t + 1], nstat[:, t:t + 1]))
                V.tensor_scalar(xN[:, t, :], xN[:, t, :], rstat[:, t:t + 1], None, ALU.mult).then_inc(x_scaled, 1)

            for t in range(NT):
                dve.wait_ge(xsum_ready, t + 1)
                root_arg(nstat[:, t:t + 1], stat[:, t:t + 1], D).then_inc(xroot_ready, 1)
                if t:
                    x_scale(t - 1)
            x_scale(NT - 1)

            ready("setup")
            b0 = bank("setup")
            V.tensor_copy(gains, b0[:, 0, 0:61])
            V.tensor_copy(posT, b0[:, 0, 64:128])
            V.tensor_copy(biasRow[:, 0:T], b0[0:16, 1, :]).then_inc(taken["V"], 1)
            for i in range(4):
                dve.wait_ge(hidden_high, i + 1)
                for b in range(2):
                    c = 2 * i + b
                    ins = rest(hTL[:, c, :], bank(("x", i))[:, b, :], hTH[:, c, :], gains[:, c:c + 1])
                ins.then_inc(taken["V"], 1)
                if i % 2:
                    low(i // 2)
            dve.wait_ge(s_pos, 32)
            link(V.tensor_copy(angle[:, :], posI[:, :]))
            link(V.tensor_scalar(angle[:, :], angle[:, :], turn[:, 0:1], None, ALU.mult))
            MAGIC = 1.5 * 2.0 ** 23
            C1 = 6.28125
            C2 = 2 * np.pi - C1
            PI = 3.1415925
            for dst, quarter in ((sinT, 0.0), (cosT, 0.25)):
                link(V.tensor_scalar(turns[:, :], angle[:, :], 1 / (2 * np.pi), quarter, ALU.mult, ALU.add))
                link(V.tensor_scalar(turns[:, :], turns[:, :], MAGIC, None, ALU.add))
                link(V.tensor_scalar(turns[:, :], turns[:, :], -MAGIC, -quarter, ALU.add, ALU.add))
                link(V.scalar_tensor_tensor(dst[:, :], turns[:, :], -C1, angle[:, :], ALU.mult, ALU.add))
                link(V.scalar_tensor_tensor(dst[:, :], turns[:, :], -C2, dst[:, :], ALU.mult, ALU.add))
                ins = V.tensor_scalar(dst[:, :], dst[:, :], PI, -PI, ALU.min, ALU.max)
            ins.then_inc(angle_ready, 1)

            def rotate(name, dst):
                ready(name)
                b = bank(name)
                V.tensor_tensor(dst[:, :], b[:, 0, :], cosT[:, :], ALU.mult)
                link(V.tensor_tensor(ropeTmp[:, :], b[:, 1, :], sinT[:, :], ALU.mult))
                V.tensor_tensor(dst[:, :], dst[:, :], ropeTmp[:, :], ALU.add).then_inc(taken["V"], 1)

            low(slab_at["lat", 0] + 2)
            low(slab_at["lat", 1] + 2)
            low(slab_at["lat", 2] + 2)
            dve.wait_ge(latsum_ready, NT)
            root_arg(nstat[:, 0:4], stat[:, 0:4], DQ)
            root_arg(nstat[:, 4:8], stat[:, 4:8], DKV).then_inc(latsum_ready, 1)
            dve.wait_ge(sine_ready, 1)
            link(V.tensor_scalar(sinT[:, :], sinT[:, :], turn[:, 1:2], None, ALU.mult))
            rotate("krope", krT)
            low(slab_at["kr",] + 2)
            dve.wait_ge(root_done, 5)
            link(V.reciprocal(rstat[:, 0:8], nstat[:, 0:8]))
            for t in range(NT):
                V.tensor_scalar(latN[:, t, 0:DQ], latN[:, t, 0:DQ], rstat[:, t:t + 1], None, ALU.mult)
                V.tensor_scalar(latN[:, t, DQ:DQ + DKV], latN[:, t, DQ:DQ + DKV], rstat[:, 4 + t:5 + t], None,
                                ALU.mult).then_inc(lat_scaled, 1)
            low(slab_at["iq", 0] + 2)
            ready(("iq", 1))
            V.tensor_copy(iqT[:, 2:4, :], bank(("iq", 1))[:, :, :]).then_inc(taken["V"], 1)
            low(slab_at["iq", 1] + 2)
            ready("ik")
            V.tensor_copy(ikT[:, :], bank("ik")[:, 0, :]).then_inc(taken["V"], 1)
            low(slab_at["ik",] + 2)
            for i in range(3):
                dve.wait_ge(lat_high, i + 1)
                for b in range(2 if i < 2 else 1):
                    c = 2 * i + b
                    ins = rest(latL[:, c, :], bank(("latT", i))[:, b, :], latH[:, c, :], gains[:, 56 + c:57 + c])
                ins.then_inc(taken["V"], 1)
            dve.wait_ge(s_strip0, 16)
            dve.wait_ge(taken["A"], taken_count[product_at["lat", 2]])
            n = 0

            def iscore_of(i):
                return iscore[:, TRI[i] - P:TRI[i] - P + (i + 1) * P]

            for i in range(1, NT):
                for h in range(8):
                    dve.wait_ge(index_taken, n + 1)
                    r = relu[:, n % 2, 0:(i + 1) * P]
                    if h == 0:
                        ins = V.tensor_scalar(iscore_of(i), r, iw[:, i, h:h + 1], None, ALU.mult)
                    else:
                        dve.wait_ge(index_added, n)
                        ins = V.scalar_tensor_tensor(iscore_of(i), r, iw[:, i, h:h + 1], iscore_of(i), ALU.mult, ALU.add)
                    ins.then_inc(index_added, 1)
                    n += 1
                dve.wait_ge(index_added, n)
                d = iscore[:, TRI[i] - P + i * P:TRI[i] - P + (i + 1) * P]
                link(V.tensor_tensor(d, d, strip0[:, T - P:], ALU.add))

            rounds = [(i, k) for i in range(1, NT) for k in range(TOPK // 8)]

            def select(first, count):
                for i, k in rounds[first:first + count]:
                    w = iscore_of(i)
                    link(V.max(top8, w))
                    link(V.match_replace(w, top8, w, FILL))
                    if k == TOPK // 8 - 1:
                        ins = V.tensor_scalar(selb[:, TRI[i] - P:TRI[i] - P + (i + 1) * P], w, FILL, NEG,
                                              ALU.not_equal, ALU.mult)
                        ins.then_inc(selection_ready, 1)

            def softmax_in(n, slot, bias_of, scale=1.0):
                for i in range(NT):
                    cols = (i + 1) * P
                    dve.wait_ge(score_ready, n + i + 1)
                    V.tensor_tensor_reduce(out=probs[:, slot, TRI[i]:TRI[i] + cols], in0=SCORE[(n + i) % 3][:, 0:cols],
                                           in1=bias_of(i, cols), scale=scale, scalar=-3.0e38, op0=ALU.add, op1=ALU.max,
                                           accum_out=rowmax[:, 4 * slot + i:4 * slot + i + 1]).then_inc(score_taken, 1)
                dve.wait_ge(score_taken, n + NT)
                V.tensor_scalar(negmax[:, 4 * slot:4 * slot + 4], rowmax[:, 4 * slot:4 * slot + 4], -1.0, None,
                                ALU.mult).then_inc(negmax_ready, 1)

            def normalise(u, slot, gate=None):
                dve.wait_ge(exp_done, u + 1)
                r = rtotal[:, 4 * slot:4 * slot + 4]
                ins = V.reciprocal(r, total[:, 4 * slot:4 * slot + 4])
                if gate is not None:
                    link(ins)
                    ins = V.tensor_tensor(r, r, gate, ALU.mult)
                link(ins)
                for i in range(NT):
                    t = probs[:, slot, TRI[i]:TRI[i] + (i + 1) * P]
                    ins = V.tensor_scalar(t, t, rtotal[:, 4 * slot + i:4 * slot + i + 1], None, ALU.mult)
                ins.then_inc(probs_ready, 1)

            def head_low(att):
                dve.wait_ge(attended_high, att + 1)
                V.tensor_tensor(oTL[:, att % 8, :], ATT[att % 2][:, :], oTH[:, att % 8, :].bitcast(F32), ALU.subtract).then_inc(attended_taken, 1)

            for p in range(4):
                s = slab_at["uq", p]
                rotate(("m2", p), qrT)
                low(s + 2)
                if p:
                    for h in range(2):
                        head_low(2 * (p - 1) + h)
                for h in range(2):
                    softmax_in((2 * p + h) * NT, h, lambda i, cols: strip0[:, T - cols:], MLA_SCALE)
                low(s + 3)
                for h in range(2):
                    normalise(2 * p + h, h)
                select(4 * p, 4)

            def merge(b):
                for n in range(GROUPS):
                    if n == 0:
                        for h in range(2):
                            head_low(8 * b + 6 + h)
                    low(slab_at["bg", b, n] + 2)
                    if b == 0:
                        select(16 + 8 * n, 4)
                    if b == 2 and n:
                        merged_low(n - 1)
                    ready(("bp", b, n))
                    dve.wait_ge(taken["A"], taken_count[product_at["bg", b, n]])
                    if b:
                        k = (b - 1) * GROUPS + n
                        if k:
                            dve.wait_ge(merge_added, k)
                        ins = V.tensor_tensor(gated[:, :, :], bank(("bp", b, n))[:, :, :], sig[:, :, :], ALU.mult)
                    else:
                        ins = V.tensor_tensor(merged[:, 2 * n:2 * n + 2, :], bank(("bp", b, n))[:, :, :], sig[:, :, :], ALU.mult)
                    ins.then_inc(taken["V"], 1)
                    low(slab_at["bp", b, n] + 2)
                    if b == 0:
                        select(20 + 8 * n, 4)

            def merged_low(n):
                dve.wait_ge(merged_high, n + 1)
                c = slice(2 * n, 2 * n + 2)
                V.tensor_tensor(mgL[:, c, :], merged[:, c, :], mgH[:, c, :].bitcast(F32), ALU.subtract).then_inc(merged_ready, 1)

            merge(0)
            for p in range(4):
                low(slab_at["dq", p] + 2)
                ready(("dk", p))
                V.tensor_copy(kT[:, :, :], bank(("dk", p))[:, :, :]).then_inc(taken["V"], 1)
                if p == 0:
                    low(slab_at["dk", p] + 2)
                else:
                    for h in range(2):
                        head_low(8 + 2 * (p - 1) + h)
                for h in range(2):
                    u = 8 + 2 * p + h
                    dve.wait_ge(strips_loaded[p % 2], 16 * (p // 2 + 1))
                    dve.wait_ge(biased_ready, 2 * p + h + 1)

                    def bias(i, cols, h=h):
                        return biased[:, h, TRI[i]:TRI[i] + cols] if i else strips[:, p % 2, h, T - cols:]
                    softmax_in(u * NT, h, bias)
                if p:
                    low(slab_at["dk", p] + 2)
                low(slab_at["dv", p] + 2)
                for h in range(2):
                    normalise(8 + 2 * p + h, h)
            merge(1)

            for t in flatH + flatL:
                V.memset(t[:, FLAT:].bitcast(F32), 0.0)
            low(slab_at["kc",] + 2)
            for kv, src in enumerate((kcT, vcT)):
                name = ("kc", "vc")[kv]
                dve.wait_ge(taken["A"], taken_count[product_at[name]])
                if kv:
                    dve.wait_ge(flat_split, 1)
                for r in range(2):
                    row = src[:, r, :]
                    window = bass.AP(row.tensor, row.offset, [row.ap[0], (1, 32), (16, NC)])
                    ins = V.tensor_tensor(flat_[:, r, :, :], window, posT[:, kv * 32:(kv + 1) * 32].unsqueeze(2).broadcast_to((P, 32, NC)), ALU.add)
                ins.then_inc(flat_ready, 1)
                dve.wait_ge(flat_high, kv + 1)
                vh, vl = (t[kv][:, 0:FLAT].rearrange("p (l c) -> p l c", c=2 * NC) for t in (flatH, flatL))
                for r in range(2):
                    f = (slice(None), slice(None), slice(r * NC, (r + 1) * NC))
                    ins = V.tensor_tensor(vl[f], flat_[:, r, :, :], vh[f].bitcast(F32), ALU.subtract)
                ins.then_inc(flat_split, 1)
            low(slab_at["vc",] + 2)

            def nsa_key(r):
                ready(("kk", r))
                V.tensor_copy(kT[:, :, :], bank(("kk", r))[:, :, :]).then_inc(taken["V"], 1)

            for name, i in NSA_BEGIN:
                if name == "kk":
                    nsa_key(i)
                if name != "vv":
                    low(slab_at[(name, *i) if name == "cw" else (name, i)] + 2)
            dve.wait_ge(cmp2_loaded, 32)
            dve.wait_ge(gates_ready, 1)
            for p in range(4):
                r = p // 2
                if p == 2:
                    low(slab_at["nq", p] + 2)
                    nsa_key(r)
                if p == 0:
                    ready("hidT")
                    V.tensor_copy(hid[:, :, :, :].rearrange("p v k c -> p (v k c)"), bank("hidT")[:, 0, 0:8 * NC]).then_inc(taken["V"], 1)
                    ready("cmp")
                    V.tensor_copy(kcmpT[:, :], bank("cmp")[:, 0, 0:2 * NC])
                    V.tensor_copy(vcmp[0:NC, :, :], bank("cmp")[0:NC, 1, 0:2 * P].rearrange("p (r c) -> p r c", c=P)).then_inc(taken["V"], 1)
                    low(slab_at["vv", 0] + 2)
                if p:
                    for h in range(2):
                        head_low(16 + 2 * (p - 1) + h)
                if p == 2:
                    low(slab_at["kk", r] + 2)
                n = TILE_NSA + NSA_TILES * p
                dve.wait_ge(strips_loaded[p % 2], 16 * (p // 2 + 3))
                for h in range(2):
                    for w in range(2):
                        softmax_in(n, 2 * h + w, lambda i, cols: strips[:, p % 2, h, T - cols:])
                        n += NT
                for h in range(2):
                    dve.wait_ge(score_ready, n + 1)
                    t = probC[:, h, :, 0:NC]
                    m = maxC[:, 4 * h:4 * h + 4]
                    V.tensor_tensor(t, SCORE[n % 3][:, 0:P].rearrange("p (t c) -> p t c", c=32)[:, :, 0:NC], late[:, :, :], ALU.add).then_inc(score_taken, 1)
                    n += 1
                    dve.wait_ge(score_taken, n)
                    link(V.tensor_reduce(m, t, AX, ALU.max))
                    link(V.tensor_scalar(m, m, -1e20, None, ALU.max))
                    V.tensor_tensor(t, t, m.unsqueeze(2).broadcast_to((P, NT, NC)), ALU.subtract).then_inc(cmpmax_ready, 1)
                if p:
                    low((slab_at["nq", p] if p % 2 else slab_at["vv", r]) + 2)
                for h in range(2):
                    for w in range(2):
                        u = 2 * h + w
                        c = (1 + w) * 8 + 2 * p + h
                        normalise(16 + 4 * p + u, u, gateN[:, :, c])
                for h in range(2):
                    dve.wait_ge(cmpexp_done, 2 * p + h + 1)
                    m, s_, q = (x[:, 4 * h:4 * h + 4] for x in (maxC, totC, rC))
                    link(V.tensor_reduce(s_, probC[:, h, :, 0:NC], AX, ALU.add))
                    link(V.tensor_scalar(m, s_, 0.0, None, ALU.is_equal))
                    link(V.tensor_tensor(s_, s_, m, ALU.add))
                    link(V.reciprocal(q, s_))
                    link(V.tensor_tensor(q, q, gateN[:, :, 2 * p + h], ALU.mult))
                    t = probC[:, h, :, 0:NC]
                    V.tensor_tensor(t, t, q.unsqueeze(2).broadcast_to((P, NT, NC)), ALU.mult).then_inc(probs_ready, 1)
            merge(2)

            for i in range(1, 4, 2):
                if i == 3:
                    low(slab_at["wo", 0] + 2)
                ready(("xt", i))
                V.tensor_copy(XT[:, 2 * i:2 * i + 2, :], bank(("xt", i))[:, :, :]).then_inc(taken["V"], 1)
                if i == 1:
                    merged_low(GROUPS - 1)
            dve.wait_ge(memsum_ready, 2)
            root_arg(nstat[:, 0:2], stat[:, 0:2], D).then_inc(memroot_ready, 1)
            dve.wait_ge(root_done, 6)
            link(V.reciprocal(rstat[:, 0:2], nstat[:, 0:2]))
            for t in range(2):
                V.tensor_scalar(memN[:, t, :], memN[:, t, :], rstat[:, t:t + 1], None, ALU.mult).then_inc(mem_scaled, 1)

            def post(j, gain):
                dve.wait_ge(rms_ready, 2 * j + 1)
                link(V.reciprocal(rstd[:, :], rstd[:, :]))
                for c in range(KD):
                    V.scalar_tensor_tensor(yT[:, c, :], yT[:, c, :], gains[:, gain * KD + c:gain * KD + c + 1], rstd[:, :],
                                           ALU.mult, ALU.mult).then_inc(post_scaled[j], 1)
                    if c % 2 and j:
                        dve.wait_ge(post_scaled[j], c + 1)
                        V.tensor_tensor(XT[:, c, :], XT[:, c, :], yT[:, c, :], ALU.add).then_inc(resid_dve[j], 1)

            def cross_key(n):
                ready(("ck", n))
                V.tensor_copy(kxT[:, 2 * n:2 * n + 2, :], bank(("ck", n))[:, :, 0:MEM]).then_inc(taken["V"], 1)
                low(slab_at["ck", n] + 2)

            def pre(j, gain):
                dve.wait_ge(rms_ready, 2 * j + 2)
                link(V.reciprocal(rstd[:, :], rstd[:, :]))

                for c in range(KD):
                    if j == 0 and c in (2, 4):
                        cross_key(1 + c // 2)
                    if j == 0 and c == 6:
                        low(slab_at["cv", 0] + 2)
                    if c >= 2:
                        dve.wait_ge(nhid_ready[j], c - 1)
                    V.scalar_tensor_tensor(normed[:, c % 2, :], XT[:, c, :], gains[:, gain * KD + c:gain * KD + c + 1], rstd[:, :],
                                           ALU.mult, ALU.mult).then_inc(normed_ready[j], 1)

            for i in range(2):
                low(slab_at["wo", i + 1] + 2)
                dve.wait_ge(mem_high, i + 1)
                for c in range(4):
                    k = 4 * i + c
                    ins = rest(memL[:, k, :], S[c // 2][:, c % 2 * MEM:(c % 2 + 1) * MEM], memH[:, k, :], gains[:, 24 + k:25 + k])
                ins.then_inc(mem_taken, 1)
            low(slab_at["wo", GROUPS - 1] + 2)
            post(0, 1)
            for n in range(2):
                cross_key(n)
            pre(0, 2)
            for n in range(1, GROUPS):
                low(slab_at["cv", n] + 2)

            def cross_low(n):
                for b in range(2):
                    c = 2 * n + b
                    dve.wait_ge(catt_high, c + 1)
                    V.tensor_tensor(coL[:, c, :], (OT, S[1])[b][:, :], coH[:, c, :].bitcast(F32), ALU.subtract).then_inc(catt_taken, 1)

            for n in range(GROUPS):
                if n:
                    cross_low(n - 1)
                for i in range(NT):
                    m = n * NT + i
                    dve.wait_ge(cross_ready, m + 1)
                    V.tensor_reduce(negmax[:, i:i + 1], S[m % 2][:, 0:MEM], AX, ALU.max, negate=True).then_inc(cmax_ready, 1)
                dve.wait_ge(cross_taken, NT * (n + 1))
                V.reciprocal(rtotal[:, 0:4], total[:, 0:4]).then_inc(crt_ready, 1)
                low(slab_at["cq", n] + 2)
            cross_low(3)
            for n in range(GROUPS - 1):
                low(slab_at["co", n] + 2)
            post(1, 4)
            low(slab_at["co", GROUPS - 1] + 2)
            pre(1, 5)

            def up_low(n):
                dve.wait_ge(up_high, n + 1)
                c = slice(2 * (n % 8), 2 * (n % 8) + 2)
                V.tensor_tensor(h1L[:, c, :], h1[:, n % 2, :, :], h1H[:, c, :].bitcast(F32), ALU.subtract).then_inc(up_ready, 1)

            for f in range(2):
                for n in range(8):
                    low(slab_at["up", f, n] + 2)
                    if n:
                        up_low(8 * f + n - 1)
                up_low(8 * f + 7)
                for n in range(GROUPS):
                    s = slab_at["down", f, n, 0]
                    low(s + 2)
                    if f:
                        ready(("down", f, n))
                        y = yT[:, 2 * n:2 * n + 2, :]
                        V.tensor_tensor(y, bank(("down", f, n))[:, :, :], y, ALU.add).then_inc(taken["V"], 1)
                    low(s + 3)
            post(2, 6)

        @block.gpsimd
        def _(pool):
            Q = nc.gpsimd
            adds = [0]
            pool.wait_ge(taken["V"], 1)
            pool.dma_start(scratch, biasRow[:, :].unsqueeze(1).broadcast_to((16, P, T + P))).then_inc(scratch_written, 16)

            def load_strips(k):
                src = bass.AP(scratch.tensor, 2 * k * P * (T + P) + P - 1, [(T + P - 1, P), (P * (T + P), 2), (1, T)])
                pool.dma_start(strips[:, k % 2, :, :], src).then_inc(strips_loaded[k % 2], 16)

            pool.wait_ge(scratch_written, 16)
            pool.wait_ge(product_ready, ready_at["m4", 3])
            load_strips(0)
            load_strips(1)
            pool.wait_ge(selection_ready, NT - 1)
            for p in range(4):
                if p:
                    pool.wait_ge(score_taken, (UNITS_MLA + 2 * p) * NT)
                    if p < 3:
                        load_strips(p + 1)
                pool.wait_ge(strips_loaded[p % 2], 16 * (p // 2 + 1))
                for h in range(2):
                    for i in range(1, NT):
                        cols = (i + 1) * P
                        ins = Q.tensor_tensor(biased[:, h, TRI[i]:TRI[i] + cols], strips[:, p % 2, h, T - cols:],
                                              selb[:, TRI[i] - P:TRI[i] - P + cols], ALU.add)
                    ins.then_inc(biased_ready, 1)

            def merge(b):
                for n in range(GROUPS):
                    if b == 2 and n == GROUPS - 1:
                        pool.wait_ge(product_ready, ready_at["bp", 2, n])
                        pool.dma_start(memN[:, :, :], out_row(a["mem"])).then_inc(mem_loaded, 16)
                    pool.wait_ge(taken["V"], taken_count[product_at["bp", b, n]])
                    m = merged[:, 2 * n:2 * n + 2, :]
                    Q.tensor_tensor(m, m, gated[:, :, :], ALU.add).then_inc(merge_added, 1)

            merge(1)
            pool.wait_ge(product_ready, ready_at["hid", 1])
            load_strips(4)
            load_strips(5)
            for p in range(4):
                if p < 2:
                    pool.wait_ge(score_taken, TILE_NSA + NSA_TILES * (p + 1))
                    load_strips(6 + p)
            pool.wait_ge(attended_taken, 24)
            pool.dma_start(xN2[:, :, :], out_row(a["x"])).then_inc(x2_loaded, 16)
            merge(2)
            Q.memset(ones[:, :], 1.0).then_inc(ones_ready, 1)

            def hidden_low(j):
                for c in range(KD):
                    pool.wait_ge(nhigh_ready[j], c + 1)
                    Q.tensor_tensor(hTL[:, c, :], normed[:, c % 2, :], hTH[:, c, :].bitcast(F32), ALU.subtract).then_inc(nhid_ready[j], 1)

            def add_squares(j, ready):
                for n in range(GROUPS - 1):
                    pool.wait_ge(ready, n + 1 + GROUPS * (j % 2))
                    q = outSquare[j][:, n % 2, :, :]
                    if n:
                        adds[0] += 1
                        Q.tensor_tensor(squareSum[:, :], squareSum[:, :], q[:, 0, :], ALU.add).then_inc(pool_step, 1)
                        pool.wait_ge(pool_step, adds[0])
                        Q.tensor_tensor(squareSum[:, :], squareSum[:, :], q[:, 1, :], ALU.add).then_inc(squares_added, 1)
                    else:
                        Q.tensor_tensor(squareSum[:, :], q[:, 0, :], q[:, 1, :], ALU.add).then_inc(squares_added, 1)
                    pool.wait_ge(squares_added, (GROUPS - 1) * j + n + 1)

            def residual(j):
                for c in range(0, KD, 2 if j else 1):
                    pool.wait_ge(post_scaled[j], c + 1)
                    Q.tensor_tensor(XT[:, c, :], XT[:, c, :], yT[:, c, :], ALU.add).then_inc(resid_ready[j], 1)

            pool.wait_ge(taken["A"], taken_count[product_at["xt", 2]])
            pool.wait_ge(taken["V"], taken_count[product_at["xt", 3]])
            pool.wait_ge(product_ready, ready_at["xt", 3])
            add_squares(0, squared)
            residual(0)
            hidden_low(0)
            for n in range(GROUPS):
                pool.wait_ge(crt_ready, n + 1)
                for i in range(NT):
                    ins = Q.tensor_scalar(probX[:, i, :], probX[:, i, :], rtotal[:, i:i + 1], None, ALU.mult)
                ins.then_inc(cprobs_ready, 1)
            add_squares(1, squared)
            residual(1)
            hidden_low(1)
            for n in range(16):
                pool.wait_ge(taken["A"], taken_count[product_at["up", n // 8, n % 8]])
                t = h1[:, n % 2, :, :]
                Q.tensor_tensor(t, t, t, ALU.mult).then_inc(up_squared, 1)
            add_squares(2, downsq_ready)
            residual(2)


INS = ("x", "mem", "positions", "rel_bias", "norm_gains", "w_in", "mla_q_norm", "mla_kv_norm", "mla_w_uq",
       "mla_w_ukv", "nsa_cmp_pos", "nsa_cmp_w1", "nsa_cmp_w2", "w_branch", "w_out", "cross_wq", "cross_wkv",
       "cross_wo", "mlp_w1", "mlp_w2")


def kernel(**inputs):
    import concourse.bacc as bacc
    from concourse.bass_utils import run_bass_kernel_spmd

    nc = bacc.Bacc("TRN2", target_bir_lowering=False, num_devices=1)
    given = {name: np.ascontiguousarray(inputs[name]) for name in INS}
    given.update(shape_constants())
    aps = {name: nc.dram_tensor(f"in_{name}", v.shape, mybir.dt.from_np(v.dtype), kind="ExternalInput").ap()
           for name, v in given.items()}
    out = nc.dram_tensor("out", (1, T, D), F32, kind="ExternalOutput").ap()
    layer(nc, aps, out)
    r = run_bass_kernel_spmd(nc, [{f"in_{name}": v for name, v in given.items()}], core_ids=[0])
    return r.results[0]["out"]
```
